# Optimizing a Trainium2 kernel written in Bass

```python
import jax, jax.numpy as jnp
from jax import lax
import numpy as np

"""One inference step of a hybrid decoder trunk (YOCO-style dual path), run for a prompt group
and a sample group with the same weights.
Layer 0 (mixer A): multi-scale causal pooling mixer + SwiGLU FFN.
Layer 1 (mixer B): multi-head latent attention reading ONE shared compressed latent and decoupled
rotary key, computed from the residual stream after layer 0, followed by a SwiGLU FFN.
Post-LayerNorm with DeepNorm residual scaling. 16 learned meta tokens are prepended to prompts.

Inputs:
  x_prompt   (BATCH, SEQ, D_MODEL)
  x_sample   (DEC_BATCH, DEC_SEQ, D_MODEL)
  state_pool (N_A_LAYERS, DEC_BATCH, POOL_HIST, D_MODEL)  last 15 input rows of each pooling mixer
  cache_ckv  (N_POOL_PAGES, PAGE_SIZE, KV_LORA)            paged shared latent (after its RMSNorm)
  cache_kpe  (N_POOL_PAGES, PAGE_SIZE, QK_ROPE)            paged shared rotary key (rotated)
  page_table (DEC_BATCH, PAST_LEN // PAGE_SIZE) int32
Returned tuple:
  y_prompt    (BATCH, SEQ, D_MODEL)
  y_sample    (DEC_BATCH, DEC_SEQ, D_MODEL)
  pool_prompt (N_A_LAYERS, BATCH, POOL_HIST, D_MODEL)
  pool_sample (N_A_LAYERS, DEC_BATCH, POOL_HIST, D_MODEL)
  ckv_prompt  (BATCH, SEQ + N_META, KV_LORA)      latent rows for positions 0..SEQ+15 (meta included)
  kpe_prompt  (BATCH, SEQ + N_META, QK_ROPE)
  ckv_sample  (DEC_BATCH, DEC_SEQ, KV_LORA)       latent rows for positions PAST_LEN..
  kpe_sample  (DEC_BATCH, DEC_SEQ, QK_ROPE)
"""

D_MODEL = 1024
BATCH = 1
SEQ = 1024
DEPTH = 2
DEC_BATCH = 8
DEC_SEQ = 1
PAST_LEN = 4096
PAGE_SIZE = 128

N_META = 16
N_A_LAYERS = DEPTH // 2
N_B_LAYERS = DEPTH - N_A_LAYERS
POOL_WINDOWS = (2, 4, 8, 16)
N_POOL_GROUPS = len(POOL_WINDOWS)
POOL_GROUP = D_MODEL // N_POOL_GROUPS
POOL_HIST = max(POOL_WINDOWS) - 1
N_HEADS = 8
QK_NOPE = 128
QK_ROPE = 64
V_HEAD = 128
Q_LORA = 384
KV_LORA = 256
ROPE_THETA = 10000.0
D_FF = -(-8 * D_MODEL // (3 * 256)) * 256
ALPHA = (2 * DEPTH) ** 0.25
BETA = (8 * DEPTH) ** -0.25
Q_BLOCK = 128
LN_EPS = 1e-5
RMS_EPS = 1e-6
SM_SCALE = (QK_NOPE + QK_ROPE) ** -0.5

kernel_name = "yoco_pool_mla_decoder_step"

def _layer_norm(x, g, b):
    xf = x.astype(jnp.float32)
    mu = xf.mean(-1, keepdims=True)
    var = jnp.square(xf - mu).mean(-1, keepdims=True)
    y = (xf - mu) * lax.rsqrt(var + LN_EPS) * g.astype(jnp.float32) + b.astype(jnp.float32)
    return y.astype(x.dtype)

def _rms_norm(x, g):
    xf = x.astype(jnp.float32)
    y = xf * lax.rsqrt(jnp.square(xf).mean(-1, keepdims=True) + RMS_EPS) * g.astype(jnp.float32)
    return y.astype(x.dtype)

def _rope(x, pos):
    half = QK_ROPE // 2
    inv = ROPE_THETA ** (-jnp.arange(half, dtype=jnp.float32) / half)
    ang = pos.astype(jnp.float32)[:, None] * inv[None, :]
    shp = (pos.shape[0],) + (1,) * (x.ndim - 3) + (half,)
    cos, sin = jnp.cos(ang).reshape(shp), jnp.sin(ang).reshape(shp)
    xf = x.astype(jnp.float32)
    x1, x2 = xf[..., :half], xf[..., half:]
    return jnp.concatenate([x1 * cos - x2 * sin, x2 * cos + x1 * sin], axis=-1).astype(x.dtype)

def _pool_mixer(x, hist, w, scale):
    p_len, n_new = hist.shape[1], x.shape[1]
    xs = jnp.concatenate([hist, x], axis=1)
    j = jnp.arange(p_len, p_len + n_new)
    outs = []
    for g, win in enumerate(POOL_WINDOWS):
        xg = xs[..., g * POOL_GROUP:(g + 1) * POOL_GROUP].astype(jnp.float32)
        c = jnp.concatenate([jnp.zeros_like(xg[:, :1]), jnp.cumsum(xg, axis=1)], axis=1)
        lo = jnp.maximum(j - win + 1, 0)
        cnt = (j + 1 - lo).astype(jnp.float32)
        outs.append((c[:, j + 1] - c[:, lo]) / cnt[None, :, None] - xg[:, p_len:])
    d = jnp.stack(outs, axis=2).astype(x.dtype)
    y = jnp.einsum('blgc,gce->blge', d, w).reshape(x.shape)
    return y * scale

def _swiglu(x, w_gate, w_up, w_down):
    return (jax.nn.silu(x @ w_gate) * (x @ w_up)) @ w_down

def _shared_latent(x, pos, wkv_a, kv_norm):
    kv = x @ wkv_a
    ckv = _rms_norm(kv[..., :KV_LORA], kv_norm)
    kpe = _rope(kv[..., KV_LORA:], pos)
    return ckv, kpe

def _mla_query(x, pos, wq_a, q_norm, wq_b, wkv_b):
    bsz, n = x.shape[:2]
    q = (_rms_norm(x @ wq_a, q_norm) @ wq_b).reshape(bsz, n, N_HEADS, QK_NOPE + QK_ROPE)
    q_pe = _rope(q[..., QK_NOPE:], pos)
    q_lat = jnp.einsum('blhn,rhn->blhr', q[..., :QK_NOPE], wkv_b[:, :, :QK_NOPE])
    return q_lat, q_pe

def _latent_attention(q_lat, q_pe, q_pos, ckv_past, kpe_past, ckv_new, kpe_new):
    bsz, nq = q_lat.shape[:2]
    n_past = ckv_past.shape[1]
    k_pos = jnp.arange(n_past + ckv_new.shape[1])
    blk = min(Q_BLOCK, nq)
    nb = -(-nq // blk)
    pad = nb * blk - nq

    def blocks(t):
        t = jnp.pad(t, ((0, 0), (0, pad)) + ((0, 0),) * (t.ndim - 2))
        return jnp.moveaxis(t.reshape((bsz, nb, blk) + t.shape[2:]), 1, 0)

    ql_b, qp_b = blocks(q_lat), blocks(q_pe)
    pos_b = jnp.pad(q_pos, (0, pad), mode='edge').reshape(nb, blk)

    def one(args):
        ql, qp, qpos = args

        def scores(ckv, kpe):
            return jnp.einsum('bqhr,bkr->bhqk', ql, ckv) + jnp.einsum('bqhp,bkp->bhqk', qp, kpe)

        s = jnp.concatenate([scores(ckv_past, kpe_past), scores(ckv_new, kpe_new)], axis=-1)
        s = s.astype(jnp.float32) * SM_SCALE
        s = jnp.where(k_pos[None, :] <= qpos[:, None], s, -jnp.inf)
        p = jax.nn.softmax(s, axis=-1).astype(ckv_new.dtype)
        return (jnp.einsum('bhqk,bkr->bqhr', p[..., :n_past], ckv_past)
                + jnp.einsum('bhqk,bkr->bqhr', p[..., n_past:], ckv_new))

    o = lax.map(one, (ql_b, qp_b, pos_b))
    o = jnp.moveaxis(o, 0, 1).reshape((bsz, nb * blk) + o.shape[3:])
    return o[:, :nq]

def _trunk(x, pos0, pool_hist, ckv_past, kpe_past, ln_g, ln_b, pool_w, pool_scale,
           w_gate, w_up, w_down, wq_a, q_norm, wq_b, wo, wkv_a, kv_norm, wkv_b):
    bsz, n = x.shape[:2]
    pos = pos0 + jnp.arange(n)
    new_pool = []
    ckv_new = kpe_new = None
    for l in range(DEPTH):
        if l < N_A_LAYERS:
            hist = pool_hist[l]
            new_pool.append(jnp.concatenate([hist, x], axis=1)[:, -POOL_HIST:])
            h = _pool_mixer(x, hist, pool_w[l], pool_scale[l])
        else:
            b = l - N_A_LAYERS
            if ckv_new is None:
                ckv_new, kpe_new = _shared_latent(x, pos, wkv_a, kv_norm)
            q_lat, q_pe = _mla_query(x, pos, wq_a[b], q_norm[b], wq_b[b], wkv_b)
            o = _latent_attention(q_lat, q_pe, pos, ckv_past, kpe_past, ckv_new, kpe_new)
            h = jnp.einsum('blhr,rhv->blhv', o, wkv_b[:, :, QK_NOPE:]).reshape(bsz, n, N_HEADS * V_HEAD) @ wo[b]
        x = _layer_norm(ALPHA * x + h, ln_g[l, 0], ln_b[l, 0])
        x = _layer_norm(ALPHA * x + _swiglu(x, w_gate[l], w_up[l], w_down[l]), ln_g[l, 1], ln_b[l, 1])
    return x, jnp.stack(new_pool), ckv_new, kpe_new

def setup_inputs(seed: int = 0) -> dict:
    key = jax.random.key(seed)
    ks = jax.random.split(key, 24)
    n_pages = PAST_LEN // PAGE_SIZE
    n_used = DEC_BATCH * n_pages
    n_pool_pages = n_used + n_used // 4

    def nrm(k, shape, scale):
        return jax.random.normal(k, shape, jnp.float32) * scale

    page_table = jax.random.permutation(ks[5], n_pool_pages)[:n_used].reshape(DEC_BATCH, n_pages).astype(jnp.int32)
    return {
        'x_prompt': nrm(ks[0], (BATCH, SEQ, D_MODEL), 1.0),
        'x_sample': nrm(ks[1], (DEC_BATCH, DEC_SEQ, D_MODEL), 1.0),
        'state_pool': nrm(ks[2], (N_A_LAYERS, DEC_BATCH, POOL_HIST, D_MODEL), 1.0),
        'cache_ckv': nrm(ks[3], (n_pool_pages, PAGE_SIZE, KV_LORA), 1.0),
        'cache_kpe': nrm(ks[4], (n_pool_pages, PAGE_SIZE, QK_ROPE), 1.0),
        'page_table': page_table,
        'meta_tokens': nrm(ks[6], (N_META, D_MODEL), 1.0),
        'ln_g': 1.0 + nrm(ks[7], (DEPTH, 2, D_MODEL), 0.01),
        'ln_b': nrm(ks[8], (DEPTH, 2, D_MODEL), 0.01),
        'pool_w': nrm(ks[9], (N_A_LAYERS, N_POOL_GROUPS, POOL_GROUP, POOL_GROUP), POOL_GROUP ** -0.5 * BETA),
        'pool_scale': 1.0 + nrm(ks[10], (N_A_LAYERS, D_MODEL), 0.1),
        'w_gate': nrm(ks[11], (DEPTH, D_MODEL, D_FF), D_MODEL ** -0.5),
        'w_up': nrm(ks[12], (DEPTH, D_MODEL, D_FF), D_MODEL ** -0.5),
        'w_down': nrm(ks[13], (DEPTH, D_FF, D_MODEL), D_FF ** -0.5 * BETA),
        'wq_a': nrm(ks[14], (N_B_LAYERS, D_MODEL, Q_LORA), D_MODEL ** -0.5),
        'q_norm': 1.0 + nrm(ks[15], (N_B_LAYERS, Q_LORA), 0.01),
        'wq_b': nrm(ks[16], (N_B_LAYERS, Q_LORA, N_HEADS * (QK_NOPE + QK_ROPE)), Q_LORA ** -0.5),
        'wo': nrm(ks[17], (N_B_LAYERS, N_HEADS * V_HEAD, D_MODEL), (N_HEADS * V_HEAD) ** -0.5 * BETA),
        'wkv_a': nrm(ks[18], (D_MODEL, KV_LORA + QK_ROPE), D_MODEL ** -0.5),
        'kv_norm': 1.0 + nrm(ks[19], (KV_LORA,), 0.01),
        'wkv_b': nrm(ks[20], (KV_LORA, N_HEADS, QK_NOPE + V_HEAD), KV_LORA ** -0.5),
    }

def reference(x_prompt, x_sample, state_pool, cache_ckv, cache_kpe, page_table, meta_tokens,
              ln_g, ln_b, pool_w, pool_scale, w_gate, w_up, w_down,
              wq_a, q_norm, wq_b, wo, wkv_a, kv_norm, wkv_b):
    weights = (ln_g, ln_b, pool_w, pool_scale, w_gate, w_up, w_down,
               wq_a, q_norm, wq_b, wo, wkv_a, kv_norm, wkv_b)

    bsz = x_prompt.shape[0]
    meta = jnp.broadcast_to(meta_tokens.astype(x_prompt.dtype)[None], (bsz, N_META, D_MODEL))
    xp = jnp.concatenate([meta, x_prompt], axis=1)
    empty_hist = [jnp.zeros((bsz, 0, D_MODEL), xp.dtype) for _ in range(N_A_LAYERS)]
    yp, pool_prompt, ckv_prompt, kpe_prompt = _trunk(
        xp, 0, empty_hist,
        jnp.zeros((bsz, 0, KV_LORA), xp.dtype), jnp.zeros((bsz, 0, QK_ROPE), xp.dtype),
        *weights)
    y_prompt = yp[:, N_META:]

    dbsz, n_pages = page_table.shape
    past_len = n_pages * PAGE_SIZE
    ckv_past = cache_ckv[page_table].reshape(dbsz, past_len, KV_LORA)
    kpe_past = cache_kpe[page_table].reshape(dbsz, past_len, QK_ROPE)
    hist = [state_pool[i] for i in range(N_A_LAYERS)]
    y_sample, pool_sample, ckv_sample, kpe_sample = _trunk(
        x_sample, past_len, hist, ckv_past, kpe_past, *weights)

    return (y_prompt, y_sample, pool_prompt, pool_sample, ckv_prompt, kpe_prompt, ckv_sample, kpe_sample)


_drawn_inputs = setup_inputs


def setup_inputs(seed=0):
    import zlib

    import numpy as np

    out = dict(_drawn_inputs(seed))
    spreads = {}
    factors = {'cache_ckv': 5.899,
     'cache_kpe': 8.0,
     'ln_g': 2.744,
     'ln_b': 2.685,
     'q_norm': 8.0,
     'kv_norm': 5.781}
    for name, (base, spread) in spreads.items():
        noise = np.random.default_rng([zlib.crc32(name.encode()), seed]).standard_normal(out[name].shape)
        drawn = base * np.exp(spread * noise) if base else spread * noise
        out[name] = __import__('jax').numpy.asarray(drawn.astype(out[name].dtype))
    for name, factor in factors.items():
        out[name] = (out[name] * factor).astype(out[name].dtype)
    return out
```

```python
from contextlib import ExitStack

import numpy as np

import concourse.bass as bass
from concourse import mybir
from concourse.alu_op_type import AluOpType as ALU

F32 = mybir.dt.float32
F32R = mybir.dt.float32r
I32 = mybir.dt.int32
ACT = mybir.ActivationFunctionType
AX = mybir.AxisListType

P = 128
BANK = 512
LO = 64
WINDOWS = (2, 4, 8, 16)
ROPE_THETA = 10000.0
LN_EPS, RMS_EPS = 1e-5, 1e-6
MASKED = -1e30
DEPTH = 2
ALPHA = float((2 * DEPTH) ** 0.25)


def rope_angles(pos, half):
    inv = (ROPE_THETA ** (-np.arange(half) / half)).astype(np.float32)
    ang = (np.asarray(pos, np.float32)[:, None] * inv[None, :]).astype(np.float32).astype(np.float64)
    return np.cos(ang).astype(np.float32), np.sin(ang).astype(np.float32)


class Layout:

    def __init__(self, parts):
        self.at, n = {}, 0
        for name, width in parts:
            self.at[name] = (n, width)
            n += width
        self.width = n


KEPT = Layout([("ident", P), ("mask", P + 16), ("same_head", 72), ("fold", 8), ("row_in_block", 1),
               ("rope_sample", 2), ("one", 1)])


def bands_layout(nt):
    g = len(WINDOWS)
    return Layout([("here", g * P), ("before", g * P), ("meta_before", g * P), ("hist", g * nt),
                   ("meta", g * nt)])


def kept_constants(n_heads, n_samples, past, half, scale):
    c = np.zeros((P, KEPT.width), np.float32)

    def put(name, a):
        o, w = KEPT.at[name]
        c[:a.shape[0], o:o + a.shape[1]] = a

    put("ident", np.eye(P, dtype=np.float32))
    q, k = np.arange(P)[:, None], np.arange(P + 16)[None, :]
    put("mask", np.where(k <= q, 0.0, MASKED).astype(np.float32))
    rows = np.arange(64)
    same = np.zeros((64, 72), np.float32)
    for m in range(8):
        same[rows % n_heads == m, m] = 1.0
        same[rows % n_heads == m, LO + m] = 1.0
    put("same_head", same)
    fold = np.zeros((72, 8), np.float32)
    fold[np.arange(8), np.arange(8)] = 1.0
    fold[LO + np.arange(8), np.arange(8)] = 1.0
    put("fold", fold)
    put("row_in_block", (np.arange(P) % 32).astype(np.float32)[:, None])
    cos, sin = rope_angles([past], half)
    two = np.stack([np.tile(cos[0], 4), np.tile(np.concatenate([-sin[0], sin[0]]), 2)], 1)
    put("rope_sample", two)
    put("one", np.ones((P, 1), np.float32))
    return c


def band_constants(ns, nm):
    nt = ns + nm
    lay = bands_layout(nt)
    c = np.zeros((P, lay.width), np.float32)
    s, t = np.arange(P)[:, None], np.arange(P)[None, :]
    for g, w in enumerate(WINDOWS):
        def put(name, a):
            o, full = lay.at[name]
            n = full // len(WINDOWS)
            c[:a.shape[0], o + g * n:o + g * n + a.shape[1]] = a
        d = t - s
        put("here", np.where((d >= 0) & (d < w), 1.0 / w, 0.0) - (d == 0))
        put("before", np.where(d + P < w, 1.0 / w, 0.0))
        dm = t - (s[:nt] - ns - nm)
        put("meta_before", np.where((s[:nt] >= ns) & (dm < w), 1.0 / w, 0.0))
        b, j = s // 16, s % 16
        col = np.arange(nt)[None, :]
        put("hist", np.where((col < ns) & (b == col), np.where(j >= 16 - w, 1.0 / w, 0.0) - (j == 15), 0.0))
        si, ti = np.arange(nt)[:, None] - ns, np.arange(nt)[None, :] - ns
        dd = ti - si
        cnt = np.minimum(ti + 1, w)
        inside = (si >= 0) & (ti >= 0)
        put("meta", np.where(inside, np.where((dd >= 0) & (dd < w), 1.0 / np.maximum(cnt, 1), 0.0) - (dd == 0), 0.0))
    return c


def rope_rows(seq, ns, nm, past, half):
    tiles = seq // P
    out = np.zeros((P, tiles + 1, 4 * half), np.float32)
    cos, sin = rope_angles(nm + np.arange(seq), half)
    all4 = np.concatenate([cos, cos, -sin, sin], 1)
    out[:, :tiles] = all4.reshape(tiles, P, 4 * half).transpose(1, 0, 2)
    cos, sin = rope_angles([past] * ns + list(range(nm)), half)
    out[:ns + nm, tiles] = np.concatenate([cos, cos, -sin, sin], 1)
    return out.reshape(P, -1)


def rope_columns(seq, nm, half, scale):
    cos, sin = rope_angles(nm + np.arange(seq), half)
    c = np.tile((cos * np.float32(scale)).T, (4, 1))
    s = np.tile(np.concatenate([-(sin * np.float32(scale)).T, (sin * np.float32(scale)).T], 0), (2, 1))
    return np.stack([c, s], 1).astype(np.float32).reshape(P, -1)


class Sems:
    STAGES = ("mix", "ffn0", "att", "ffn1")

    def __init__(self, ctx, nc, tiles, steps):
        self.ctx, self.nc, self.made = ctx, nc, {}
        rows = tiles + 1
        every = {n: rows for n in ("stats", "root", "scale", "normed", "gained", "rows")}
        every.update({n: 2 * tiles + 1 for n in ("turned", "turned_hi", "turned_lo")})
        every.update(gain_in=32, norm_steps=7 * rows + 2, unit_done=2 * rows, unit_taken=2 * rows)
        ffn = dict(every, unit_done=2 * rows * steps, unit_taken=2 * rows * steps, steps=3 * steps - 2, x_scaled=rows)
        ffn.update({"raw_in%d" % i: 2 * 16 * steps for i in range(3)})
        ffn.update({n: 6 * steps for n in ("w_hi", "w_lo")})
        ffn.update({n: 4 * steps for n in ("gu_done", "silu", "h_mul", "h_hi", "h_lo")})
        ffn.update({"tail_" + n: steps for n in ("done", "sum", "silu", "mul", "turned", "hi", "lo")})
        self.totals = {"mix": every, "ffn0": ffn, "att": every, "ffn1": ffn}

    def shared(self, name):
        stage, _, rest = name.partition("_")
        if stage not in self.STAGES:
            return name, 0
        before = self.STAGES[:self.STAGES.index(stage)]
        return rest, sum(self.totals[b].get(rest, 0) for b in before)

    def __getitem__(self, name):
        name, _ = self.shared(name)
        if name not in self.made:
            self.made[name] = self.ctx.enter_context(self.nc.semaphore(name))
        return self.made[name]

    def at(self, name, n):
        return self[name], self.shared(name)[1] + n


class Chain:

    def __init__(self, eng, sem, base=0):
        self.eng, self.sem, self.base, self.n = eng, sem, base, 0

    def link(self, ins):
        ins.then_inc(self.sem, 1)
        self.n += 1
        self.eng.wait_ge(self.sem, self.base + self.n)


def wait_apart(eng, k):
    eng.sem_inc(k.s["apart"], 1)


def hi_part(act, hi, src, scale=1.0):
    return act.activation(hi, src, ACT.Copy, scale=scale)


def lo_part(dve, lo, src, hi, scale=None):
    if scale is None:
        return dve.tensor_tensor(lo, src, hi.bitcast(F32), ALU.subtract)
    return dve.scalar_tensor_tensor(out=lo, in0=src, scalar=scale, in1=hi.bitcast(F32),
                                    op0=ALU.mult, op1=ALU.subtract)


def product(pe, out, still, moving, start, stop):
    pe.matmul(out, still[0], moving[0], start=start, stop=False)
    pe.matmul(out, still[0], moving[1], start=False, stop=False)
    return pe.matmul(out, still[1], moving[0], start=False, stop=stop)


def product_tail(pe, out, still, moving, start, stop):
    pe.matmul(out, still, moving[0], start=start, stop=False)
    return pe.matmul(out, still, moving[1], start=False, stop=stop)


class Shared:

    def __init__(self, a):
        self.x_prompt, self.x_sample, self.state_pool = a["x_prompt"], a["x_sample"], a["state_pool"]
        self.cache_ckv, self.cache_kpe, self.page_table = a["cache_ckv"], a["cache_kpe"], a["page_table"]
        self.meta_tokens, self.ln_g, self.ln_b = a["meta_tokens"], a["ln_g"], a["ln_b"]
        self.pool_w, self.pool_scale, self.w_gate = a["pool_w"], a["pool_scale"], a["w_gate"]
        self.w_up, self.w_down, self.wq_a = a["w_up"], a["w_down"], a["wq_a"]
        self.q_norm, self.wq_b, self.wkv_a = a["q_norm"], a["wq_b"], a["wkv_a"]
        self.kv_norm, self.wkv_b, self.in_kept = a["kv_norm"], a["wkv_b"], a["in_kept"]
        self.in_bands, self.in_rope_rows, self.in_rope_cols = a["in_bands"], a["in_rope_rows"], a["in_rope_cols"]
        self.y_prompt, self.y_sample, self.pool_prompt = a["y_prompt"], a["y_sample"], a["pool_prompt"]
        self.pool_sample, self.ckv_prompt, self.kpe_prompt = a["pool_sample"], a["ckv_prompt"], a["kpe_prompt"]
        self.ckv_sample, self.kpe_sample = a["ckv_sample"], a["kpe_sample"]
        self.wo_w = a["wo"]


UNIT_BANKS = (4, 5, 6)


def rows_of(k, t, nt):
    return k.x_main[:, t, :] if t < k.tiles else k.x_tail[0:nt, :]


def unit_bank(u):
    return UNIT_BANKS[u % 3]


def pe_unit_free(pe, k, ph, u):
    if not isinstance(u, int) or u >= 3:
        pe.wait_ge(*k.s.at(ph + "_unit_taken", u - 2))


def dve_add_unit(dve, k, ph, u, t, e, nt, scaled, chain):
    s = k.s
    dve.wait_ge(*s.at(ph + "_unit_done", u + 1))
    row = rows_of(k, t, nt)[:, e * BANK:(e + 1) * BANK]
    ps = k.ps[:, unit_bank(2 * t + e), :]

    def add(part):
        if scaled:
            return dve.scalar_tensor_tensor(out=row, in0=row, scalar=ALPHA, in1=part, op0=ALU.mult, op1=ALU.add)
        return dve.tensor_tensor(row, row, part, ALU.add)

    if t < k.tiles:
        add(ps).then_inc(s[ph + "_unit_taken"], 1)
        return
    chain.link(add(ps[0:nt]))
    dve.tensor_tensor(row, row, ps[LO:LO + nt], ALU.add).then_inc(s[ph + "_unit_taken"], 1)


def dve_row_stats(dve, k, ph, t, nt, chain, taken):
    s, n = k.s, (P if t < k.tiles else nt)
    row = rows_of(k, t, nt)
    dve.wait_ge(*s.at(ph + "_unit_taken", taken))
    st = k.stats[:, t % 2]
    for e in range(2):
        ins = dve.bn_stats(st[0:n, e, :], row[:, e * BANK:(e + 1) * BANK])
        if e == 0:
            ins.then_inc(chain.sem, 1)
            chain.n += 1
    chain.link(ins)
    dve.bn_aggr(k.mean_var[0:n, t, :], st[0:n]).then_inc(s[ph + "_stats"], 1)


def act_root(act, k, ph, t, nt):
    n = P if t < k.tiles else nt
    act.wait_ge(*k.s.at(ph + "_stats", t + 1))
    act.activation(k.root[0:n, t:t + 1], k.mean_var[0:n, t, 1:2], ACT.Sqrt, bias=k.ln_eps[0:n, 0:1],
                   scale=1.0).then_inc(k.s[ph + "_root"], 1)


def newton_rsqrt(dve, r, root, var_eps, tmp, chain):
    chain.link(dve.reciprocal(r, root))
    chain.link(dve.scalar_tensor_tensor(out=tmp, in0=r, scalar=r, in1=var_eps, op0=ALU.mult, op1=ALU.mult))
    chain.link(dve.tensor_scalar(tmp, tmp, -0.5, 1.5, ALU.mult, ALU.add))
    chain.link(dve.tensor_tensor(r, r, tmp, ALU.mult))


def dve_row_scale(dve, k, ph, t, nt, chain):
    n = P if t < k.tiles else nt
    col = slice(t, t + 1)
    chain.link(dve.tensor_scalar(k.var_eps[0:n, col], k.mean_var[0:n, t, 1:2], LN_EPS, None, ALU.add))
    dve.wait_ge(*k.s.at(ph + "_root", t + 1))
    newton_rsqrt(dve, k.scale[0:n, col], k.root[0:n, col], k.var_eps[0:n, col], k.newton[0:n, col], chain)
    dve.scalar_tensor_tensor(out=k.shift[0:n, col], in0=k.mean_var[0:n, t, 0:1], scalar=-1.0,
                             in1=k.scale[0:n, col], op0=ALU.mult, op1=ALU.mult).then_inc(k.s[ph + "_scale"], 1)


def act_normalise(act, k, ph, t, nt):
    n = P if t < k.tiles else nt
    row = rows_of(k, t, nt)
    act.wait_ge(*k.s.at(ph + "_scale", t + 1))
    act.activation(row, row, ACT.Identity, bias=k.shift[0:n, t:t + 1],
                   scale=k.scale[0:n, t:t + 1]).then_inc(k.s[ph + "_normed"], 1)


def pool_gain_bias(pool, k, ph, t, nt):
    n = P if t < k.tiles else nt
    row = rows_of(k, t, nt)
    if t == 0:
        pool.wait_ge(*k.s.at(ph + "_gain_in", 32))
    pool.wait_ge(*k.s.at(ph + "_normed", t + 1))
    pool.tensor_tensor(row, row, k.gain[0:n, :], ALU.mult).then_inc(k.s[ph + "_gained"], 1)
    pool.wait_ge(*k.s.at(ph + "_gained", t + 1))
    pool.tensor_tensor(row, row, k.bias[0:n, :], ALU.add).then_inc(k.s[ph + "_rows"], 1)


def sp_load_gain(sp, k, ph, layer, which):
    sp.dma_start(k.gain[:, :], k.ln_g[layer, which, :].partition_broadcast(P)).then_inc(k.s[ph + "_gain_in"], 16)
    sp.dma_start(k.bias[:, :], k.ln_b[layer, which, :].partition_broadcast(P)).then_inc(k.s[ph + "_gain_in"], 16)


TURN_BANKS = 3


def turn_bank(k, t, b):
    if t >= k.tiles - 1:
        return 7 if t == k.tiles else 2 + b
    return (2 * t + b) % TURN_BANKS


def pe_turn(pe, k, ph, t, nt):
    s = k.s
    pe.wait_ge(*s.at(ph + "_rows", t + 1))
    row = rows_of(k, t, nt)
    if t < k.tiles:
        for b in range(2):
            if 2 * t + b >= TURN_BANKS:
                pe.wait_ge(*s.at(ph + "_turned_lo", 2 * t + b + 1 - TURN_BANKS))
            for j in range(4):
                mm = pe.transpose(k.ps[:, turn_bank(k, t, b), j * P:(j + 1) * P],
                                  row[:, (4 * b + j) * P:(4 * b + j + 1) * P], k.ident)
            mm.then_inc(s[ph + "_turned"], 1)
    else:
        pe.wait_ge(*s.at(ph + "_turned_lo", 2 * t + 1 - TURN_BANKS))
        for j in range(k.kc):
            mm = pe.transpose(k.ps[:, turn_bank(k, t, 0), j * nt:(j + 1) * nt], row[:, j * P:(j + 1) * P],
                              k.ident[0:nt, 0:nt])
        mm.then_inc(s[ph + "_turned"], 1)


def turned_parts(k, t, nt):
    if t < k.tiles:
        for b in range(2):
            cols = slice(t * P, (t + 1) * P)
            src = k.ps[:, turn_bank(k, t, b), :].rearrange("p (j n) -> p j n", j=4)
            yield 2 * t + b, src, k.xt_hi[:, 4 * b:4 * b + 4, cols], k.xt_lo[:, 4 * b:4 * b + 4, cols]
    else:
        src = k.ps[:, turn_bank(k, t, 0), 0:k.kc * nt].rearrange("p (j n) -> p j n", j=k.kc)
        yield 2 * t, src, k.xt_tail[:, :, 0:nt], k.xt_tail[:, :, LO:LO + nt]


def act_turned_hi(act, k, ph, t, nt):
    for n, src, hi, _ in turned_parts(k, t, nt):
        act.wait_ge(*k.s.at(ph + "_turned", n + 1))
        hi_part(act, hi, src).then_inc(k.s[ph + "_turned_hi"], 1)


def dve_turned_lo(dve, k, ph, t, nt):
    for n, src, hi, lo in turned_parts(k, t, nt):
        dve.wait_ge(*k.s.at(ph + "_turned_hi", n + 1))
        lo_part(dve, lo, src, hi).then_inc(k.s[ph + "_turned_lo"], 1)


def pe_norm_stage(pe, k, ph, nt, units, turn, between=None):
    for step in range(k.tiles + 4):
        if step <= k.tiles:
            units(step)
        if between is not None:
            between(step)
        if turn and 3 <= step:
            pe_turn(pe, k, ph, step - 3, nt)


def act_norm_stage(act, k, ph, nt, turn, extra=None):
    for step in range(k.tiles + 4):
        if extra is not None:
            extra(step)
        if turn and 3 <= step:
            act_turned_hi(act, k, ph, step - 3, nt)
        if step <= k.tiles:
            act_root(act, k, ph, step, nt)
        if 1 <= step <= k.tiles + 1:
            act_normalise(act, k, ph, step - 1, nt)


def dve_norm_stage(dve, k, ph, nt, turn, scaled, unit0=0, extra=None):
    chain = Chain(dve, *k.s.at(ph + "_norm_steps", 0))
    for step in range(k.tiles + 5):
        if turn and 4 <= step:
            dve_turned_lo(dve, k, ph, step - 4, nt)
        if extra is not None:
            extra(step)
        if step <= k.tiles:
            t = step
            for e in range(2):
                dve_add_unit(dve, k, ph, unit0 + 2 * t + e, t, e, nt, scaled, chain)
            dve_row_stats(dve, k, ph, t, nt, chain, unit0 + 2 * t + 2)
        if 1 <= step <= k.tiles + 1:
            dve_row_scale(dve, k, ph, step - 1, nt, chain)


def pool_norm_stage(pool, k, ph, nt):
    for t in range(k.tiles + 1):
        pool_gain_bias(pool, k, ph, t, nt)


def mixer_sp(sp, k):
    s = k.s
    nt = k.ns + k.nm
    sp.dma_start(k.kept[:, :], k.in_kept).then_inc(s["kept_in"], 16)
    sp.dma_start(k.pages, k.page_table.rearrange("b n -> (b n)").partition_broadcast(P)).then_inc(s["pages_in"], 16)
    sp.dma_start(k.bands[:, :], k.in_bands).then_inc(s["bands_in"], 16)
    sp.dma_start(k.x_tail[k.ns:nt, :], k.meta_tokens).then_inc(s["tail_in"], 16)
    sp.dma_start(k.x_tail[0:k.ns, :], k.x_sample[:, 0, :]).then_inc(s["tail_in"], 16)
    x = k.x_prompt[0].rearrange("(t p) d -> p t d", p=P)
    for t in range(k.tiles):
        sp.dma_start(k.x_main[:, t, :], x[:, t, :]).then_inc(s["x_in%d" % t], 16)
        if t == 0:
            sp.dma_start(k.pool_raw[:, :, :],
                         k.pool_w[0].rearrange("g (h p) e -> p (g h) e", p=P)).then_inc(s["pool_w_in"], 16)
            sp.dma_start(k.pool_gain[:, :], k.pool_scale[0, :].partition_broadcast(P)).then_inc(s["pool_w_in"], 16)
    for b in range(k.ns):
        sp.dma_start(k.hist[16 * b:16 * b + 15, :], k.state_pool[0, b]).then_inc(s["hist_in"], 16)
    sp.dma_start(k.hist[15:P:16, :], k.x_sample[:, 0, :]).then_inc(s["hist_in"], 16)
    sp_load_gain(sp, k, "mix", 0, 0)
    sp.dma_start(k.pool_prompt[0, 0], k.x_prompt[0, k.seq - 15:k.seq, :]).then_inc(s["stored"], 16)
    sp.dma_start(k.pool_sample[0, :, 0:14, :], k.state_pool[0, :, 1:15, :]).then_inc(s["stored"], 16)
    sp.dma_start(k.pool_sample[0, :, 14, :], k.x_sample[:, 0, :]).then_inc(s["stored"], 16)
    k.n_stored += 3


def mixer_fold_gain(eng, k):
    chain = Chain(eng, k.s["pool_fold_steps"])
    eng.wait_ge(k.s["pool_w_in"], 32)
    for h in range(2):
        ins = eng.tensor_tensor(k.pool_raw[:, h:k.kc:2, :], k.pool_raw[:, h:k.kc:2, :],
                                k.pool_gain[:, :].rearrange("p (g e) -> p g e", g=4), ALU.mult)
        chain.link(ins)


POOLED_BANKS = (7, 3)


def first_gate_up(k, pe, layer):
    def between(step):
        if step == k.tiles + 2:
            k.ffn[layer].first_product(pe)
    return between


def first_weights(k, eng, layer, act):
    def extra(step):
        if step == k.tiles - 2:
            k.ffn[layer].split_first(eng, act)
    return extra


def mixer_pe(pe, k):
    s, nt = k.s, k.ns + k.nm
    pe.wait_ge(s["kept_in"], 16)
    pe.wait_ge(s["bands_in"], 16)
    pe.wait_ge(s["tail_in"], 32)

    def pool_half(t, half):
        n = 2 * t + half
        if half == 0 and t < k.tiles:
            pe.wait_ge(s["x_in%d" % t], 16)
        if half == 0 and t == k.tiles:
            pe.wait_ge(s["hist_in"], 16 * (k.ns + 1))
        if n >= 2:
            pe.wait_ge(s["pooled_lo"], n - 1)
        for j in range(4):
            kc = 4 * half + j
            g, cols = kc // 2, slice(kc * P, (kc + 1) * P)
            if t < k.tiles:
                out = k.ps[:, POOLED_BANKS[half], j * P:(j + 1) * P]
                pe.matmul(out, k.x_main[:, t, cols], k.pool_band("here", g), start=True, stop=False)
                if t:
                    mm = pe.matmul(out, k.x_main[:, t - 1, cols], k.pool_band("before", g), start=False, stop=True)
                else:
                    mm = pe.matmul(out, k.x_tail[0:nt, cols], k.pool_band("meta_before", g)[0:nt], start=False, stop=True)
            else:
                out = k.ps[:, POOLED_BANKS[half], j * nt:(j + 1) * nt]
                pe.matmul(out, k.hist[:, cols], k.pool_band("hist", g), start=True, stop=False)
                mm = pe.matmul(out, k.x_tail[0:nt, cols], k.pool_band("meta", g)[0:nt], start=False, stop=True)
        mm.then_inc(s["pooled"], 1)

    def unit(t, e):
        u = 2 * t + e
        if u == 0:
            pe.wait_ge(s["pool_w_lo"], 2)
        pe.wait_ge(s["pooled_lo"], 2 * t + 1 + e)
        pe_unit_free(pe, k, "mix", u)
        for g in (2 * e, 2 * e + 1):
            cols = slice((g % 2) * 256, (g % 2 + 1) * 256)
            for h in range(2):
                kc = 2 * g + h
                w = (k.pool_hi[:, kc, :], k.pool_lo[:, kc, :])
                if t < k.tiles:
                    mm = product(pe, k.ps[:, unit_bank(u), cols],
                                 (k.pooled_hi[:, t % 2, kc, :], k.pooled_lo[:, t % 2, kc, :]), w, h == 0, h == 1)
                else:
                    mm = product_tail(pe, k.ps[0:LO + nt, unit_bank(u), cols], k.pooled_tail[:, kc, 0:LO + nt],
                                      w, h == 0, h == 1)
        mm.then_inc(s["mix_unit_done"], 1)

    pool_half(0, 0)
    pool_half(0, 1)

    def units(t):
        for e in range(2):
            if t < k.tiles:
                pool_half(t + 1, e)
            unit(t, e)

    pe_norm_stage(pe, k, "mix", nt, units, True, first_gate_up(k, pe, 0))


def pooled_parts(k, t, half):
    nt = k.ns + k.nm
    if t < k.tiles:
        src = k.ps[:, POOLED_BANKS[half], :].rearrange("p (j n) -> p j n", j=4)
        return (src, k.pooled_hi[:, t % 2, 4 * half:4 * half + 4, :], k.pooled_lo[:, t % 2, 4 * half:4 * half + 4, :])
    src = k.ps[:, POOLED_BANKS[half], 0:4 * nt].rearrange("p (j n) -> p j n", j=4)
    return (src, k.pooled_tail[:, 4 * half:4 * half + 4, 0:nt], k.pooled_tail[:, 4 * half:4 * half + 4, LO:LO + nt])


def mixer_act(act, k):
    s = k.s

    def pooled(t):
        for half in range(2):
            act.wait_ge(s["pooled"], 2 * t + half + 1)
            if 2 <= t < k.tiles:
                act.wait_ge(*s.at("mix_unit_done", 2 * t - 2))
            src, hi, _ = pooled_parts(k, t, half)
            hi_part(act, hi, src).then_inc(s["pooled_hi"], 1)

    pooled(0)
    for n in range(2):
        act.wait_ge(s["pool_fold_steps"], 2)
        hi_part(act, k.pool_hi[:, 4 * n:4 * n + 4, :], k.pool_raw[:, 4 * n:4 * n + 4, :]).then_inc(s["pool_w_hi"], 1)
    weights = first_weights(k, act, 0, True)

    def extra(step):
        if step < k.tiles:
            pooled(step + 1)
        weights(step)

    act_norm_stage(act, k, "mix", k.ns + k.nm, True, extra)


def mixer_dve(dve, k):
    s = k.s

    def pooled(t):
        for half in range(2):
            dve.wait_ge(s["pooled_hi"], 2 * t + half + 1)
            src, hi, lo = pooled_parts(k, t, half)
            lo_part(dve, lo, src, hi).then_inc(s["pooled_lo"], 1)

    dve.memset(k.ln_eps[:, :], LN_EPS).then_inc(s["zeroed"], 1)
    dve.memset(k.rms_eps[:, :], RMS_EPS).then_inc(s["zeroed"], 1)
    pooled(0)
    mixer_fold_gain(dve, k)
    for n in range(2):
        dve.wait_ge(s["pool_w_hi"], n + 1)
        lo_part(dve, k.pool_lo[:, 4 * n:4 * n + 4, :], k.pool_raw[:, 4 * n:4 * n + 4, :],
                k.pool_hi[:, 4 * n:4 * n + 4, :]).then_inc(s["pool_w_lo"], 1)
    weights = first_weights(k, dve, 0, False)

    def extra(step):
        if step < k.tiles:
            pooled(step + 1)
        weights(step)

    dve_norm_stage(dve, k, "mix", k.ns + k.nm, True, True, extra=extra)


def mixer_pool(pool, k):
    pool.wait_ge(k.s["block_ready"], 4)
    pool.memset(k.q_all, 0.0).then_inc(k.s["pads"], 1)
    pool.memset(k.pooled_tail.bitcast(F32), 0.0).then_inc(k.s["pads"], 1)
    pool.memset(k.xt_tail.bitcast(F32), 0.0).then_inc(k.s["pads"], 1)
    pool.memset(k.h_tail.bitcast(F32), 0.0).then_inc(k.s["pads"], 1)
    pool_norm_stage(pool, k, "mix", k.ns + k.nm)


class Ffn:
    def __init__(self, k, layer, nt):
        self.k, self.layer, self.nt, self.ph = k, layer, nt, "ffn%d" % layer
        self.steps = k.ff // (2 * P)
        self.x_ph = ("mix", "att")[layer]

    def name(self, name):
        return self.ph + "_" + name

    def s(self, name):
        return self.k.s[self.name(name)]

    TAIL_AFTER = 3

    def steps_of(self, eng, body, last):
        body(0, 0)
        with eng.Fori(0, (self.steps - 3) // 2) as j:
            body(2 * j + 1, 1)
            body(2 * j + 2, 0)
        for st in range(self.steps - 2, self.steps):
            body(st, st % 2)
        last()

    def raw(self, i):
        return self.k.raw[:, i % 3, :]

    def wgu(self, st, c_slot, m, part):
        if self.layer == 1 and isinstance(st, int) and st == 0 and c_slot == 0:
            return self.k.wgu_first[:, m, part]
        return self.k.wgu[:, c_slot, m, part]

    def split_first(self, eng, act):
        for m in range(2):
            hi, lo = (self.wgu(0, 0, m, q).rearrange("p c n -> p (c n)") for q in range(2))
            self.split_tile(eng, 0, m, hi, lo, act)

    def sp(self, sp):
        k = self.k

        def tile(st, i, src):
            if self.layer == 0 and isinstance(st, int) and st == 0:
                if i == 0:
                    sp.wait_ge(k.s["pool_w_lo"], 2)
                if i == 2:
                    sp.wait_ge(k.s["pooled"], 2 * k.tiles + 2)
            if not (isinstance(st, int) and 6 * st + i < 3):
                sp.wait_ge(*self.k.s.at(self.name("w_lo"), 6 * st + i - 2))
            sp.dma_start(src[0], src[1]).then_inc(self.s("raw_in%d" % (i % 3)), 16)

        def gate_up(c, m, i):
            w = (k.w_gate, k.w_up)[m]
            return (self.raw(i).rearrange("p (c n) -> p c n", c=k.kc),
                    w[self.layer].rearrange("(c p) f -> p c f", p=P)[:, :, bass.ts(c, P)])

        def down(c, i):
            return self.raw(i), k.w_down[self.layer][bass.ts(c, P), :]

        def body(st, par):
            if isinstance(st, int) and st == 0:
                plan = [("g", 0), ("g", 1), ("g", 2)]
            elif isinstance(st, int) and st == self.steps - 1:
                plan = [("g", 2 * st + 1), ("d", 2 * st - 2), ("d", 2 * st)]
            else:
                plan = [("g", 2 * st + 1), ("d", 2 * st - 2), ("g", 2 * st + 2)]
            for n, (kind, c) in enumerate(plan):
                for m in range(2):
                    i = 2 * n + m
                    tile(st, i, gate_up(c, m, i) if kind == "g" else down(c + m, i))

        self.steps_of(sp, body, lambda: sp_load_gain(sp, k, self.ph, self.layer, 1))

    def latent_products(self, pe):
        def between(step):
            if step >= self.k.tiles + 2:
                latent_unit(pe, self.k, step - self.k.tiles - 2)
        return between if self.layer == 0 else None

    def latent_weights(self, eng, step, act):
        if self.layer == 0 and step == 3:
            for n in range(4):
                latent_split(eng, self.k, n, act)

    def split_tile(self, eng, st, i, hi, lo, act):
        if act:
            eng.wait_ge(*self.k.s.at(self.name("raw_in%d" % (i % 3)), 16 * (2 * st + i // 3 + 1)))
            hi_part(eng, hi, self.raw(i)).then_inc(self.s("w_hi"), 1)
        else:
            eng.wait_ge(*self.k.s.at(self.name("w_hi"), 6 * st + i + 1))
            lo_part(eng, lo, self.raw(i), hi).then_inc(self.s("w_lo"), 1)

    def split_gate_up(self, eng, st, i, c, slot, act):
        if act and not (isinstance(c, int) and c < 2):
            eng.wait_ge(*self.k.s.at(self.name("gu_done"), 2 * c - 2))
            if slot == 0:
                eng.wait_ge(*self.k.s.at(self.name("tail_done"), c // 2 if isinstance(c, int) else st + (i == 4)))
        for m in range(2):
            hi, lo = (self.k.wgu[:, slot, m, q].rearrange("p c n -> p (c n)") for q in range(2))
            self.split_tile(eng, st, i + m, hi, lo, act)

    def split_down(self, eng, st, i, group, act):
        if act and not (isinstance(group, int) and group < 1):
            eng.wait_ge(*self.k.s.at(self.name("unit_done"), 18 * group))
        for m in range(2):
            self.split_tile(eng, st, i + m, self.k.wd[:, 0, m, :], self.k.wd[:, 1, m, :], act)

    def weights(self, eng, st, chunk_slot, act):
        first = isinstance(st, int) and st == 0
        last = isinstance(st, int) and st == self.steps - 1
        if chunk_slot == 0:
            if first:
                self.split_gate_up(eng, 0, 2, 1, 1, act)
            else:
                self.split_gate_up(eng, st, 0, 2 * st + 1, 1, act)
                self.split_down(eng, st, 2, st - 1, act)
        elif not last:
            self.split_gate_up(eng, st, 4, 2 * st + 2, 0, act)

    def gate_up(self, pe, st, slot, hf):
        k, ps = self.k, self.k.ps
        c = 2 * st + slot
        if isinstance(st, int) and st == 0 and slot == 0:
            pe.wait_ge(*k.s.at(self.x_ph + "_turned_lo", 2 * (k.tiles - 1) if hf == 0 else 2 * k.tiles))
        if hf == 0:
            ready = (2 + 2 * slot) if isinstance(st, int) and st == 0 else 6 * st + 2 * slot
            pe.wait_ge(*self.k.s.at(self.name("w_lo"), ready))
        if not (isinstance(c, int) and c == 0):
            pe.wait_ge(*self.k.s.at(self.name("h_mul"), 2 * c + hf - 1))
        cols = slice(hf * BANK, (hf + 1) * BANK)
        for m in range(2):
            for kc in range(k.kc):
                mm = product(pe, ps[:, 2 * hf + m, :], (self.wgu(st, slot, m, 0)[:, kc, :], self.wgu(st, slot, m, 1)[:, kc, :]),
                             (k.xt_hi[:, kc, cols], k.xt_lo[:, kc, cols]), kc == 0, kc == k.kc - 1)
        mm.then_inc(self.s("gu_done"), 1)

    def first_product(self, pe):
        self.gate_up(pe, 0, 0, 0)

    def pe(self, pe):
        k, nt, ps = self.k, self.nt, self.k.ps

        def tail(st):
            if isinstance(st, int) and st == 0:
                pe.wait_ge(*k.s.at(self.x_ph + "_turned_lo", 17))
            else:
                pe.wait_ge(*self.k.s.at(self.name("tail_lo"), st))
            apart = self.layer == 1 and isinstance(st, int) and st == 0
            for m in range(2):
                for slots in ((0, 1), (1, 2)) if apart else ((0, 2),):
                    out = ps[0:LO + nt, 7, m * 256 + slots[0] * P:m * 256 + slots[1] * P]
                    for kc in range(k.kc):
                        w = [self.wgu(st, slots[0], m, q)[:, kc, :] if apart else k.wgu[:, :, m, q, kc, :]
                             for q in range(2)]
                        mm = product_tail(pe, out, k.xt_tail[:, kc, 0:LO + nt], w, kc == 0, kc == k.kc - 1)
            mm.then_inc(self.s("tail_done"), 1)

        def tail_turn(st):
            pe.wait_ge(*self.k.s.at(self.name("tail_mul"), st + 1))
            wait_apart(pe, k)
            for c in range(2):
                mm = pe.transpose(ps[:, 7, c * nt:(c + 1) * nt], k.tail_h[0:nt, c * P:(c + 1) * P], k.ident[0:nt, 0:nt])
            mm.then_inc(self.s("tail_turned"), 1)

        def down(group, par, t):
            if t == 0:
                pe.wait_ge(*self.k.s.at(self.name("h_lo"), 4 * group + 4))
                pe.wait_ge(*self.k.s.at(self.name("tail_lo"), group + 1))
                pe.wait_ge(*self.k.s.at(self.name("w_lo"), 6 * group + 10 if not (isinstance(group, int) and group == self.steps - 1)
                           else 6 * self.steps))
            for e in range(2):
                u = 18 * group + 2 * t + e
                pe_unit_free(pe, k, self.ph, u)
                out = ps[:, unit_bank(2 * t + e), :]
                cols = slice(e * BANK, (e + 1) * BANK)
                for c in range(2):
                    w = (k.wd[:, 0, c, cols], k.wd[:, 1, c, cols])
                    if t < k.tiles:
                        rows = slice(t * P, (t + 1) * P)
                        mm = product(pe, out, (k.h[:, par, 0, c, rows], k.h[:, par, 1, c, rows]), w, c == 0, c == 1)
                    else:
                        mm = product_tail(pe, out[0:LO + nt], k.h_tail[:, par, c, 0:LO + nt], w, c == 0, c == 1)
                mm.then_inc(self.s("unit_done"), 1)

        def gate_up(st, slot, hf):
            self.gate_up(pe, st, slot, hf)

        def body(st, par):
            for slot in range(2):
                if not (isinstance(st, int) and st == 0 and slot == 0):
                    gate_up(st, slot, 0)
                if slot == 1:
                    tail(st)
                gate_up(st, slot, 1)
            if isinstance(st, int) and st == 0:
                tail_turn(st)
                return
            for t in range(k.tiles + 1):
                down(st - 1, 1 - par, t)
                if t == self.TAIL_AFTER:
                    tail_turn(st)

        last = self.steps - 1
        self.steps_of(pe, body, lambda: pe_norm_stage(pe, k, self.ph, nt, lambda t: down(last, last % 2, t),
                                                      self.layer == 0, self.latent_products(pe)))

    def act(self, act):
        k, nt = self.k, self.nt

        def silu(st, slot, hf):
            n = 4 * st + 2 * slot + hf
            act.wait_ge(*self.k.s.at(self.name("gu_done"), n + 1))
            if not (isinstance(n, int) and n < 2):
                act.wait_ge(*self.k.s.at(self.name("h_mul"), n - 1))
            act.activation(k.silu[:, hf, :], k.ps[:, 2 * hf, :], ACT.Silu).then_inc(self.s("silu"), 1)

        def hidden_hi(st, slot, hf, par):
            act.wait_ge(*self.k.s.at(self.name("h_mul"), 4 * st + 2 * slot + hf + 1))
            if not (isinstance(st, int) and st < 2) and slot == 0 and hf == 0:
                act.wait_ge(*self.k.s.at(self.name("unit_done"), 18 * (st - 1)))
            hi_part(act, k.h[:, par, 0, slot, hf * BANK:(hf + 1) * BANK], k.hidden[:, hf, :]).then_inc(self.s("h_hi"), 1)

        def body(st, par):
            if self.layer == 1 and isinstance(st, int) and st == 0:
                act.wait_ge(*k.s.at("att_unit_done", 2 * (k.tiles + 1)))
            for slot in range(2):
                self.weights(act, st, slot, True)
                silu(st, slot, 0)
                hidden_hi(st, slot, 0, par)
                silu(st, slot, 1)
                hidden_hi(st, slot, 1, par)
                if slot == 1:
                    act.wait_ge(*self.k.s.at(self.name("tail_sum"), st + 1))
                    act.activation(k.tail_silu[0:nt, :], k.tail_gu[0:nt, 0:256], ACT.Silu).then_inc(self.s("tail_silu"), 1)
            if isinstance(st, int) and st == 0:
                for t in range(k.tiles + 1):
                    row = rows_of(k, t, nt)
                    act.wait_ge(*k.s.at(self.x_ph + "_turned", 17))
                    act.activation(row, row, ACT.Copy, scale=ALPHA).then_inc(self.s("x_scaled"), 1)
            act.wait_ge(*self.k.s.at(self.name("tail_turned"), st + 1))
            src = k.ps[:, 7, 0:2 * nt].rearrange("p (c n) -> p c n", c=2)
            hi_part(act, k.h_tail[:, par, :, 0:nt], src).then_inc(self.s("tail_hi"), 1)

        def last():
            self.split_down(act, self.steps - 1, 4, self.steps - 1, True)
            act_norm_stage(act, k, self.ph, nt, self.layer == 0, lambda step: self.latent_weights(act, step, True))

        self.steps_of(act, body, last)

    def dve(self, dve):
        k, nt = self.k, self.nt

        def mul(st, slot, hf):
            n = 4 * st + 2 * slot + hf
            dve.wait_ge(*self.k.s.at(self.name("silu"), n + 1))
            if not (isinstance(n, int) and n < 2):
                dve.wait_ge(*self.k.s.at(self.name("h_lo"), n - 1))
            dve.tensor_tensor(k.hidden[:, hf, :], k.silu[:, hf, :], k.ps[:, 2 * hf + 1, :], ALU.mult)\
               .then_inc(self.s("h_mul"), 1)

        def hidden_lo(st, slot, hf, par):
            dve.wait_ge(*self.k.s.at(self.name("h_hi"), 4 * st + 2 * slot + hf + 1))
            cols = slice(hf * BANK, (hf + 1) * BANK)
            lo_part(dve, k.h[:, par, 1, slot, cols], k.hidden[:, hf, :], k.h[:, par, 0, slot, cols])\
                .then_inc(self.s("h_lo"), 1)

        def body(st, par):
            chain = Chain(dve, *k.s.at(self.name("steps"), 0 if isinstance(st, int) and st == 0 else 3 * st - 2))
            for slot in range(2):
                self.weights(dve, st, slot, False)
                mul(st, slot, 0)
                hidden_lo(st, slot, 0, par)
                if slot == 1:
                    dve.wait_ge(*self.k.s.at(self.name("tail_done"), st + 1))
                    chain.link(dve.tensor_copy(k.tail_gu[0:nt, :], k.ps[LO:LO + nt, 7, :]))
                    dve.tensor_tensor(k.tail_gu[0:nt, :], k.tail_gu[0:nt, :], k.ps[0:nt, 7, :], ALU.add)\
                       .then_inc(self.s("tail_sum"), 1)
                mul(st, slot, 1)
                hidden_lo(st, slot, 1, par)
            dve.wait_ge(*self.k.s.at(self.name("tail_silu"), st + 1))
            dve.tensor_tensor(k.tail_h[0:nt, :], k.tail_silu[0:nt, :], k.tail_gu[0:nt, 256:512], ALU.mult)\
               .then_inc(self.s("tail_mul"), 1)

            def tail_lo():
                dve.wait_ge(*self.k.s.at(self.name("tail_hi"), st + 1))
                src = k.ps[:, 7, 0:2 * nt].rearrange("p (c n) -> p c n", c=2)
                lo_part(dve, k.h_tail[:, par, :, LO:LO + nt], src, k.h_tail[:, par, :, 0:nt])\
                    .then_inc(self.s("tail_lo"), 1)

            if isinstance(st, int) and st == 0:
                tail_lo()
                return
            if isinstance(st, int) and st == 1 or not isinstance(st, int):
                dve.wait_ge(*self.k.s.at(self.name("x_scaled"), k.tiles + 1))
            for t in range(k.tiles + 1):
                for e in range(2):
                    dve_add_unit(dve, k, self.ph, 18 * (st - 1) + 2 * t + e, t, e, nt, False, chain)
                if t == self.TAIL_AFTER:
                    tail_lo()

        def last():
            self.split_down(dve, self.steps - 1, 4, self.steps - 1, False)
            dve_norm_stage(dve, k, self.ph, nt, self.layer == 0, False, unit0=18 * (self.steps - 1),
                           extra=lambda step: self.latent_weights(dve, step, False))

        self.steps_of(dve, body, last)

    def pool(self, pool):
        pool_norm_stage(pool, self.k, self.ph, self.nt)


def results_sp(sp, k):
    y = k.y_prompt[0].rearrange("(t p) d -> p t d", p=P)
    for t in range(k.tiles):
        sp.wait_ge(*k.s.at("ffn1_rows", t + 1))
        sp.dma_start(y[:, t, :], k.x_main[:, t, :]).then_inc(k.s["stored"], 16)
    sp.wait_ge(*k.s.at("ffn1_rows", k.tiles + 1))
    sp.dma_start(k.y_sample[:, 0, :], k.x_tail[0:k.ns, :]).then_inc(k.s["stored"], 16)
    k.n_stored += k.tiles + 1
    for slot in range(3):
        sp.wait_ge(k.s["lat_out%d" % slot], 16 * lat_outs(k, slot))


LAT_BLOCKS = 3


def latent_tasks(k):
    return 2 * (k.tiles + 1)


def latent_width(k, u):
    return k.kv_w if u <= k.tiles else k.q_w


def latent_sp(sp, k):
    s = k.s
    sp.wait_ge(*s.at("ffn0_w_lo", 6 * k.ffn[0].steps))
    for n in range(2 * 4):
        if n >= 4:
            sp.wait_ge(s["lat_w_lo"], n - 3)
        w, width = (k.wkv_a, k.kv_w) if n < 4 else (k.wq_a[0], k.q_w)
        sp.dma_start(k.lat_raw(n), w.rearrange("(c p) e -> p c e", p=P)[:, 2 * (n % 4):2 * (n % 4) + 2, :])\
          .then_inc(s["lat_raw_in%d" % (n % 4)], 16)
        if n == 3:
            sp.wait_ge(*s.at("ffn0_rows", k.tiles + 1))
            sp.dma_start(k.rope_rows[:, :, :], k.in_rope_rows.rearrange("p (t c) -> p t c", t=k.tiles + 1))\
              .then_inc(s["lat_tables_in"], 16)
            sp.dma_start(k.kv_gain[:, :], k.kv_norm.partition_broadcast(P)).then_inc(s["lat_tables_in"], 16)
            sp.dma_start(k.q_gain[:, :], k.q_norm[0, :].partition_broadcast(P)).then_inc(s["lat_tables_in"], 16)
    sp.dma_start(k.x_spill.rearrange("(t p) d -> p t d", p=P), k.x_main[:, :, :]).then_inc(s["spilled"], 16)
    for t in range(k.tiles + 1):
        sp.wait_ge(s["lat_ready"], t + 1)
        row = k.lat_row[:, t % 3, :]
        if t < k.tiles:
            at = slice(k.nm + t * P, k.nm + (t + 1) * P)
            sp.dma_start(k.ckv_prompt[0, at, :], row[:, 0:k.rank]).then_inc(s["lat_out%d" % (t % 3)], 16)
            sp.dma_start(k.kpe_prompt[0, at, :], row[:, k.rank:k.rank + k.rope]).then_inc(s["lat_out%d" % (t % 3)], 16)
        else:
            ns, nt = k.ns, k.ns + k.nm
            sp.dma_start(k.ckv_prompt[0, 0:k.nm, :], row[ns:nt, 0:k.rank]).then_inc(s["lat_out%d" % (t % 3)], 16)
            sp.dma_start(k.kpe_prompt[0, 0:k.nm, :], row[ns:nt, k.rank:k.rank + k.rope]).then_inc(s["lat_out%d" % (t % 3)], 16)
            sp.dma_start(k.ckv_sample[:, 0, :], row[0:ns, 0:k.rank]).then_inc(s["lat_out%d" % (t % 3)], 16)
            sp.dma_start(k.kpe_sample[:, 0, :], row[0:ns, k.rank:k.rank + k.rope]).then_inc(s["lat_out%d" % (t % 3)], 16)


def lat_outs(k, slot):
    return sum(4 if t == k.tiles else 2 for t in range(k.tiles + 1) if t % 3 == slot)


def latent_split(eng, k, n, act):
    s = k.s
    hi, lo = k.lat_w(n)
    if act:
        if n == 0:
            eng.wait_ge(*s.at("ffn0_gu_done", 4 * k.ffn[0].steps))
            eng.wait_ge(*s.at("ffn0_tail_done", k.ffn[0].steps))
        if n == 5:
            eng.wait_ge(s["lat_unit_done"], k.tiles + 1)
        eng.wait_ge(s["lat_raw_in%d" % (n % 4)], 16 * (n // 4 + 1))
        hi_part(eng, hi, k.lat_raw(n)).then_inc(s["lat_w_hi"], 1)
    else:
        eng.wait_ge(s["lat_w_hi"], n + 1)
        lo_part(eng, lo, k.lat_raw(n), hi).then_inc(s["lat_w_lo"], 1)


def latent_unit(pe, k, u):
    s, nt, half = k.s, k.ns + k.nm, k.tiles + 1
    t, w = u % half, latent_width(k, u)
    if u == 0:
        pe.wait_ge(*s.at("ffn0_unit_taken", 18 * k.ffn[0].steps))
        pe.wait_ge(s["lat_w_lo"], 4)
    if u == half:
        pe.wait_ge(s["lat_w_lo"], 8)
    if u < half:
        pe.wait_ge(*s.at("ffn0_turned_lo", min(2 * t + 2, 2 * k.tiles + 1)))
    pe_unit_free(pe, k, "lat", u)
    bank = unit_bank(u)
    for kc in range(k.kc):
        hi, lo = k.lat_w(4 * (u // half) + kc // 2)
        wt = (hi[:, kc % 2, :], lo[:, kc % 2, :])
        if t < k.tiles:
            rows = slice(t * P, (t + 1) * P)
            mm = product(pe, k.ps[:, bank, 0:w], (k.xt_hi[:, kc, rows], k.xt_lo[:, kc, rows]), wt,
                         kc == 0, kc == k.kc - 1)
        else:
            mm = product_tail(pe, k.ps[0:LO + nt, bank, 0:w], k.xt_tail[:, kc, 0:LO + nt], wt,
                              kc == 0, kc == k.kc - 1)
    mm.then_inc(s["lat_unit_done"], 1)


def latent_pe(pe, k):
    s, nt = k.s, k.ns + k.nm
    half = k.tiles + 1

    def turn(u):
        t = u % half
        pe.wait_ge(s["lat_ready"], u + 1)
        if u >= 4:
            pe.wait_ge(s["lat_lo"], u - 3)
        n = P if t < k.tiles else nt
        for b in range(LAT_BLOCKS):
            mm = pe.transpose(k.ps[:, u % 4, b * n:(b + 1) * n], k.lat_row[0:n, u % 3, b * P:(b + 1) * P],
                              k.ident[0:n, 0:n])
        mm.then_inc(s["lat_turned"], 1)

    for step in range(2, latent_tasks(k) + 3):
        if step < latent_tasks(k):
            latent_unit(pe, k, step)
        if step >= 3:
            turn(step - 3)


def latent_parts(k, u):
    half, nt = k.tiles + 1, k.ns + k.nm
    t, b0 = u % half, LAT_BLOCKS * (u // half)
    n = P if t < k.tiles else nt
    ps = k.ps[:, u % 4, 0:LAT_BLOCKS * n].rearrange("p (b n) -> p b n", b=LAT_BLOCKS)
    blocks = slice(b0, b0 + LAT_BLOCKS)
    if t < k.tiles:
        cols = slice(k.nm + t * P, k.nm + (t + 1) * P)
        return ps, k.lat[:, 0, blocks, cols], k.lat[:, 1, blocks, cols], None
    return ps[:, :, k.ns:nt], k.lat[:, 0, blocks, 0:k.nm], k.lat[:, 1, blocks, 0:k.nm], (ps[:, :, 0:k.ns], k.lat_s[:, blocks, :])


def latent_act(act, k):
    s, nt, half = k.s, k.ns + k.nm, k.tiles + 1
    for step in range(latent_tasks(k) + 3):
        u = step
        if u == half:
            for p in range(5, 8):
                latent_split(act, k, p, True)
        if u < latent_tasks(k):
            n = P if u % half < k.tiles else nt
            rms = k.rank if u < half else k.q_w
            act.wait_ge(s["lat_unit_taken"], u + 1)
            if u >= 3:
                act.wait_ge(s["lat_turned"], u - 2)
                if u - 3 < half:
                    before = sum(4 if t == k.tiles else 2 for t in range(u - 2) if t % 3 == u % 3)
                    act.wait_ge(s["lat_out%d" % (u % 3)], 16 * before)
            act.activation(k.lat_row[0:n, u % 3, 0:rms], k.lat_in[0:n, u % 2, 0:rms], ACT.Square,
                           accum_out=k.lat_ss[0:n, u:u + 1]).then_inc(s["lat_square"], 1)
            act.wait_ge(s["lat_square"], u + 1)
            act.activation(k.lat_root[0:n, u:u + 1], k.lat_ss[0:n, u:u + 1], ACT.Sqrt, bias=k.rms_eps[0:n, 0:1],
                           scale=1.0 / rms).then_inc(s["lat_root"], 1)
            if u == 4:
                latent_split(act, k, 4, True)
        if step >= 3:
            v = step - 3
            act.wait_ge(s["lat_turned"], v + 1)
            src, hi, lo, sample = latent_parts(k, v)
            if v == 0:
                act.wait_ge(s["lat_pads"], 2)
            hi_part(act, hi, src).then_inc(s["lat_hi"], 1)


def latent_dve(dve, k):
    s, nt, half = k.s, k.ns + k.nm, k.tiles + 1
    chain = Chain(dve, s["lat_steps"])

    def take(u):
        t, w = u % half, latent_width(k, u)
        dve.wait_ge(s["lat_unit_done"], u + 1)
        ps = k.ps[:, unit_bank(u), 0:w]
        if u >= 2:
            dve.wait_ge(s["lat_ready"], u - 1)
        if t < k.tiles:
            dve.tensor_copy(k.lat_in[:, u % 2, 0:w], ps).then_inc(s["lat_unit_taken"], 1)
        else:
            chain.link(dve.tensor_copy(k.lat_in[0:nt, u % 2, 0:w], ps[LO:LO + nt]))
            dve.tensor_tensor(k.lat_in[0:nt, u % 2, 0:w], k.lat_in[0:nt, u % 2, 0:w], ps[0:nt], ALU.add)\
               .then_inc(s["lat_unit_taken"], 1)

    def finish(u):
        t = u % half
        n = P if t < k.tiles else nt
        rms, gain = (k.rank, k.kv_gain) if u < half else (k.q_w, k.q_gain)
        x, out = k.lat_in[0:n, u % 2, :], k.lat_row[0:n, u % 3, :]
        col = slice(u, u + 1)
        if u == 0:
            dve.wait_ge(s["lat_tables_in"], 48)
        dve.wait_ge(s["lat_root"], u + 1)
        dve.wait_ge(s["lat_unit_taken"], u + 1)
        chain.link(dve.tensor_scalar(k.lat_var[0:n, col], k.lat_ss[0:n, col], 1.0 / rms, RMS_EPS, ALU.mult, ALU.add))
        newton_rsqrt(dve, k.lat_scale[0:n, col], k.lat_root[0:n, col], k.lat_var[0:n, col], k.lat_newton[0:n, col], chain)
        ins = dve.scalar_tensor_tensor(out=out[:, 0:rms], in0=x[:, 0:rms], scalar=k.lat_scale[0:n, col],
                                       in1=gain[0:n, 0:rms], op0=ALU.mult, op1=ALU.mult)
        if u >= half:
            ins.then_inc(s["lat_ready"], 1)
            return
        r, h = k.rank, k.rope // 2
        table = k.rope_rows[0:n, t, :]
        ins = dve.tensor_tensor(out[:, r:r + 2 * h], x[:, r:r + 2 * h], table[:, 0:2 * h], ALU.mult)
        dve.tensor_tensor(k.rope_tmp[0:n, 0:h], x[:, r + h:r + 2 * h], table[:, 2 * h:3 * h], ALU.mult)
        chain.link(dve.tensor_tensor(k.rope_tmp[0:n, h:2 * h], x[:, r:r + h], table[:, 3 * h:4 * h], ALU.mult))
        chain.link(dve.tensor_tensor(out[:, r:r + 2 * h], out[:, r:r + 2 * h], k.rope_tmp[0:n, 0:2 * h], ALU.add))
        dve.tensor_copy(out[:, r + 2 * h:r + 4 * h], out[:, r:r + 2 * h]).then_inc(s["lat_ready"], 1)

    def lo(u):
        dve.wait_ge(s["lat_hi"], u + 1)
        src, hi, lo, sample = latent_parts(k, u)
        if sample is not None:
            dve.tensor_copy(sample[1], sample[0])
        lo_part(dve, lo, src, hi).then_inc(s["lat_lo"], 1)

    for step in range(latent_tasks(k) + 4):
        if step == half:
            for p in range(5, 8):
                latent_split(dve, k, p, False)
        if step < latent_tasks(k):
            take(step)
            if step == 4:
                latent_split(dve, k, 4, False)
        if 1 <= step <= latent_tasks(k):
            finish(step - 1)
        if step >= 4:
            lo(step - 4)


def latent_pool(pool, k):
    pool.wait_ge(*k.s.at("ffn0_unit_done", 18 * k.ffn[0].steps))
    end = k.nm + k.seq
    for part in range(2):
        pool.memset(k.lat[:, part, 0:LAT_BLOCKS, end:k.keys].bitcast(F32), 0.0).then_inc(k.s["lat_pads"], 1)


UNITS = [("qn", 0, 0), ("qn", 0, 1), ("qp", 0, 0), ("kn", 0, 0), ("kn", 0, 1), ("qp", 0, 1), ("kn", 0, 2)] + \
        [("v", 0, t) for t in range(9)] + \
        [("qn", 1, 0), ("qn", 1, 1), ("kn", 1, 0), ("kn", 1, 1), ("kn", 1, 2)]
UNIT_RING = 5
NU = len(UNITS)
SCORE_BANKS = (3, 0)
EXTRA_SLOT = 8


def score_pieces(k, i):
    w = k.nm + P * (i + 1)
    n = -(-w // BANK)
    if w % n:
        w = k.keys
    return n, w // n


def fills_of(i):
    blocks = [(b, b) for b in range(i + 2)]
    if i % 2:
        blocks[-1] = (i + 1, EXTRA_SLOT)
    return [blocks[a:a + 4] for a in range(0, len(blocks), 4)]


def runs_of(fill):
    runs = []
    for place, (b, slot) in enumerate(fill):
        if runs and runs[-1][1] + runs[-1][2] == slot:
            runs[-1][2] += 1
        else:
            runs.append([place, slot, 1])
    return runs


FILLS_BEFORE = [sum(len(fills_of(m % 8)) for m in range(n)) for n in range(17)]
RUNS_BEFORE = [0]
for _n in range(16):
    for _f in fills_of(_n % 8):
        RUNS_BEFORE.append(RUNS_BEFORE[-1] + len(runs_of(_f)))
NF, NR = FILLS_BEFORE[16], RUNS_BEFORE[-1]


def heads_sp(sp, k):
    s = k.s

    def load(j):
        wq = k.wq_b[0].rearrange("(c p) e -> p c e", p=P)
        for h in range(2):
            first = 2 * k.head_q * j + k.head_q * h
            sp.dma_start(k.wq_raw[:, :, h * P:(h + 1) * P], wq[:, :, bass.ds(first, P)]).then_inc(s["pair_in"], 16)
            sp.dma_start(k.wq_raw[:, :, 2 * P + h * k.rope:2 * P + (h + 1) * k.rope],
                         wq[:, :, bass.ds(first + P, k.rope)]).then_inc(s["pair_in"], 16)
        sp.dma_start(k.wkv_raw[:, :, :],
                     k.wkv_b.rearrange("(c p) h e -> p c (h e)", p=P)[:, :, bass.ts(j, 2 * k.head_kv)])\
          .then_inc(s["pair_in"], 16)

    sp.wait_ge(s["lat_w_lo"], 8)
    load(0)
    sp.wait_ge(s["lat_ready"], latent_tasks(k))
    sp.dma_start(k.rope_cols[:, :, :], k.in_rope_cols.rearrange("p (c n) -> p c n", c=2)).then_inc(s["cols_in"], 16)
    with sp.Fori(1, k.heads // 2) as j:
        sp.wait_ge(s["pair_w_lo"], 2 * j)
        wait_apart(sp, k)
        sp.wait_ge(s["sq_done"], 2 * j - 1)
        wait_apart(sp, k)
        load(j)
    sp.wait_ge(s["pair_w_lo"], k.heads)
    sp.wait_ge(s["sq_done"], k.heads)
    sp.wait_ge(s["sq_taken"], 6 * (k.heads // 2))


def pairs_of(eng, k, pair):
    with eng.Fori(0, k.heads // 2 - 1) as j:
        pair(j, False)
    pair(k.heads // 2 - 1, True)


def heads_split(eng, k, j, act):
    s = k.s
    for n, (raw, parts) in enumerate(((k.wq_raw, k.wq), (k.wkv_raw, k.wkv))):
        if act:
            if n == 0:
                eng.wait_ge(s["pair_in"], 80 * (j + 1))
            hi_part(eng, parts[:, 0], raw).then_inc(s["pair_w_hi"], 1)
        else:
            eng.wait_ge(s["pair_w_hi"], 2 * j + n + 1)
            lo_part(eng, parts[:, 1], raw, parts[:, 0]).then_inc(s["pair_w_lo"], 1)


def unit_out(k, n):
    kind, h, t = UNITS[n]
    bank = k.ps[:, n % UNIT_RING, :]
    if kind == "qn":
        cols = slice(t * BANK, (t + 1) * BANK)
        return bank, k.qn[:, h, 0, cols], k.qn[:, h, 1, cols]
    if kind == "kn":
        w = k.keys // 3
        cols = slice(t * w, (t + 1) * w)
        return bank[:, 0:w], k.kn[:, h, 0, cols], k.kn[:, h, 1, cols]
    if kind == "v":
        return bank[:, 0:256], k.v[:, 0, t, :], k.v[:, 1, t, :]
    cols = slice(t * BANK, (t + 1) * BANK)
    return bank, k.qp[:, 0, cols], k.qp[:, 1, cols]


def heads_pe(pe, k):
    s = k.s
    pe.wait_ge(s["lat_lo"], latent_tasks(k))
    pe.wait_ge(s["extra_zero"], 2)

    def unit(j, n):
        kind, h, t = UNITS[n]
        if n == 0:
            pe.wait_ge(s["pair_w_lo"], 2 * j + 1)
        if n == 3:
            pe.wait_ge(s["pair_w_lo"], 2 * j + 2)
        if n >= UNIT_RING:
            pe.wait_ge(s["hd_unit_lo"], NU * j + n + 1 - UNIT_RING)
        out = unit_out(k, n)[0]
        if kind in ("qp", "qn"):
            chunks = range(3)
            cols = slice(k.nm + t * BANK, k.nm + (t + 1) * BANK)
            for c in chunks:
                if kind == "qn":
                    w = [k.wq[:, p, c, h * P:(h + 1) * P] for p in range(2)]
                else:
                    w = [k.wq[:, p, c, 2 * P:] for p in range(2)]
                mm = product(pe, out, w, (k.lat[:, 0, 3 + c, cols], k.lat[:, 1, 3 + c, cols]), c == 0, c == 2)
        elif kind == "kn":
            w0 = k.keys // 3
            cols = slice(t * w0, (t + 1) * w0)
            for c in range(2):
                w = [k.wkv[:, p, c, h * k.head_kv:h * k.head_kv + P] for p in range(2)]
                mm = product(pe, out, w, (k.lat[:, 0, c, cols], k.lat[:, 1, c, cols]), c == 0, c == 1)
        else:
            cols = slice(0, P) if t == 0 else slice(k.nm + (t - 1) * P, k.nm + t * P)
            for c in range(2):
                w = [k.wkv_v(p, c) for p in range(2)]
                mm = product(pe, out.rearrange("p (h e) -> p h e", h=2),
                             (k.lat[:, 0, c, cols], k.lat[:, 1, c, cols]), w, c == 0, c == 1)
        mm.then_inc(s["hd_unit_done"], 1)

    def sample_queries(j):
        out = k.ps[:, 7, :]
        for h in range(2):
            for c in range(3):
                pe.matmul(out[:, 8 * h:8 * h + 8], k.wq_raw[:, c, h * P:(h + 1) * P], k.lat_s[:, 3 + c, :],
                          start=c == 0, stop=c == 2)
        for c in range(3):
            pe.matmul(out[:, 16:24], k.wq_raw[:, c, 2 * P:], k.lat_s[:, 3 + c, :], start=c == 0, stop=c == 2)
        for h in range(2):
            for c in range(2):
                mm = pe.transpose(k.ps[:, 5, (2 * h + c) * P:(2 * h + c + 1) * P],
                                  k.wkv_raw[:, c, h * k.head_kv:h * k.head_kv + P], k.ident)
        mm.then_inc(s["sq_done"], 1)

    def sample_latent_queries(j):
        pe.wait_ge(s["sq_taken"], 6 * j + 5)
        pe.wait_ge(s["sq_copied"], 5 * j + 5)
        for h in range(2):
            for c in range(2):
                m = 2 * h + c
                mm = pe.matmul(k.ps[:, 7, 8 * m:8 * m + 8], k.key_w[:, m, :], k.sq_nope[:, h, :], start=True, stop=True)
        mm.then_inc(s["sq_done"], 1)

    def scores(j, n):
        h, i = n // 8, n % 8
        if n == 0:
            pe.wait_ge(s["hd_unit_lo"], NU * j + NU)
        if n >= 2:
            pe.wait_ge(s["exp_done"], 16 * j + n - 1)
        pieces, w = score_pieces(k, i)
        q = slice(i * P, (i + 1) * P)
        half = slice(64 * h, 64 * h + 64)
        for p in range(pieces):
            out = k.ps[:, SCORE_BANKS[i % 2] + p, 0:w]
            cols = slice(p * w, (p + 1) * w)
            product(pe, out, (k.qn[:, h, 0, q], k.qn[:, h, 1, q]), (k.kn[:, h, 0, cols], k.kn[:, h, 1, cols]), True, False)
            mm = product(pe, out, (k.qp[half, 0, q], k.qp[half, 1, q]),
                         (k.lat[half, 0, 2, cols], k.lat[half, 1, 2, cols]), False, True)
        mm.then_inc(s["s_done"], 1)

    def turn(j, n):
        i = n % 8
        pe.wait_ge(s["p_ready"], 16 * j + n + 1)
        for f, fill in enumerate(fills_of(i)):
            g = FILLS_BEFORE[n] + f
            if g >= 2:
                pe.wait_ge(s["pt_lo"], NR * j + RUNS_BEFORE[g - 1])
            for place, (b, slot) in enumerate(fill):
                c0 = 0 if b == 0 else k.nm + (b - 1) * P
                mm = pe.transpose(k.ps[:, 5 + g % 2, place * P:(place + 1) * P], k.probs[:, n % 2, c0:c0 + P], k.ident)
            mm.then_inc(s["filled"], 1)

    def values(j, n):
        h, gp = n // 8, (n % 8) // 2
        g = 4 * h + gp
        pe.wait_ge(s["pt_lo"], NR * j + RUNS_BEFORE[FILLS_BEFORE[n + 1]])
        if g:
            pe.wait_ge(s["o_copied"], 8 * j + g)
        if g == 0:
            pe.wait_ge(s["sq_taken"], 6 * j + 6)
        out = k.ps[:, 7, 0:256]
        slots = [(b, b) for b in range(2 * gp + 2)] + [(2 * gp + 2, EXTRA_SLOT)]
        cols = slice(h * P, (h + 1) * P)
        for m, (b, slot) in enumerate(slots):
            rows = slice(0, k.nm) if b == 0 else slice(0, P)
            mm = product(pe, out, (k.v[rows, 0, b, cols], k.v[rows, 1, b, cols]),
                         (k.pt[rows, 0, slot, :], k.pt[rows, 1, slot, :]), m == 0, m == len(slots) - 1)
        mm.then_inc(s["pv_done"], 1)

    def pair(j, last):
        for n in range(NU):
            unit(j, n)
            if n == 6:
                sample_queries(j)
            if n == 13:
                sample_latent_queries(j)
        for n in range(19):
            if n < 16:
                scores(j, n)
            if n >= 4 and n % 2 == 0:
                values(j, n - 3)
            if 2 <= n < 18:
                turn(j, n - 2)
        pe.wait_ge(s["exp_done"], 16 * (j + 1))
        pe.wait_ge(s["pt_lo"], NR * (j + 1))
        pe.wait_ge(s["o_copied"], 8 * (j + 1))

    pairs_of(pe, k, pair)


def heads_act(act, k):
    s = k.s

    def unit(j, n):
        kind, h, t = UNITS[n]
        src, hi, _ = unit_out(k, n)
        act.wait_ge(s["hd_unit_done"], NU * j + n + 1)
        if kind == "qp":
            for a in range(4):
                b = a ^ 1
                act.activation(k.swapped[t][32 * a:32 * a + 32, :], src[32 * b:32 * b + 32, :], ACT.Copy)\
                   .then_inc(s["swapped"], 1)
            act.wait_ge(s["qp_steps"], 6 * j + 3 * t + 3)
            hi_part(act, hi, k.rotated[t]).then_inc(s["hd_unit_hi"], 1)
            return
        hi_part(act, hi, src, k.sm_scale if kind == "qn" else 1.0).then_inc(s["hd_unit_hi"], 1)

    def sample_queries(j):
        act.wait_ge(s["sq_done"], 2 * j + 1)
        for a in range(4):
            b = a ^ 1
            act.activation(k.sq_swapped[32 * a:32 * a + 32, :], k.ps[32 * b:32 * b + 32, 7, 16:24], ACT.Copy)\
               .then_inc(s["sq_copied"], 1)
        act.activation(k.key_w.rearrange("p m n -> p (m n)"), k.ps[:, 5, :], ACT.Copy).then_inc(s["sq_copied"], 1)

    def exp(j, n):
        i = n % 8
        pieces, w = score_pieces(k, i)
        act.wait_ge(s["max_done"], 16 * j + n + 1)
        if n >= 2:
            act.wait_ge(s["filled"], NF * j + FILLS_BEFORE[n - 1])
        act.activation(k.probs[:, n % 2, 0:pieces * w].rearrange("p (c w) -> p c w", c=pieces),
                       k.ps[:, SCORE_BANKS[i % 2]:SCORE_BANKS[i % 2] + pieces, 0:w], ACT.Exp,
                       bias=k.neg_max[:, n % 2:n % 2 + 1], scale=1.0,
                       accum_out=k.row_sum[:, n % 2:n % 2 + 1]).then_inc(s["exp_done"], 1)

    def turned(j, n):
        i = n % 8
        if n % 2 == 0 and n:
            act.wait_ge(s["pv_done"], 8 * j + n // 2)
        for f, fill in enumerate(fills_of(i)):
            g = FILLS_BEFORE[n] + f
            act.wait_ge(s["filled"], NF * j + g + 1)
            for place, slot, count in runs_of(fill):
                src, hi, _ = turned_view(k, g, n, place, slot, count)
                hi_part(act, hi, src).then_inc(s["pt_hi"], 1)

    def out(j, n):
        h, gp = n // 8, (n % 8) // 2
        act.wait_ge(s["pv_done"], 8 * j + n // 2 + 1)
        act.activation(k.ot_of(j, h)[:, gp * 256:(gp + 1) * 256], k.ps[:, 7, 0:256], ACT.Copy).then_inc(s["o_copied"], 1)

    act.wait_ge(s["spilled"], 16)
    act.wait_ge(s["lat_lo"], latent_tasks(k))
    heads_split(act, k, 0, True)

    def pair(j, last):
        for n in range(NU):
            unit(j, n)
            if n == 8:
                sample_queries(j)
        for n in range(19):
            if 2 <= n < 18:
                turned(j, n - 2)
            if n < 16:
                exp(j, n)
            if n >= 4 and n % 2 == 0:
                out(j, n - 3)
            if n == 8 and not last:
                heads_split(act, k, j + 1, True)

    pairs_of(act, k, pair)


def turned_view(k, g, n, place, slot, count):
    cols = slice((n % 2) * P, (n % 2 + 1) * P)
    src = k.ps[:, 5 + g % 2, place * P:(place + count) * P].rearrange("p (b n) -> p b n", b=count)
    return src, k.pt[:, 0, slot:slot + count, cols], k.pt[:, 1, slot:slot + count, cols]


def heads_dve(dve, k):
    s = k.s

    def unit(j, n):
        kind, h, t = UNITS[n]
        src, hi, lo = unit_out(k, n)
        if kind == "qp":
            cols = slice(t * BANK, (t + 1) * BANK)
            dve.wait_ge(s["swapped"], 8 * j + 4 * t + 4)
            dve.tensor_tensor(k.rotated[t], src, k.rope_cols[:, 0, cols], ALU.mult).then_inc(s["qp_steps"], 1)
            dve.tensor_tensor(k.swapped[t], k.swapped[t], k.rope_cols[:, 1, cols], ALU.mult).then_inc(s["qp_steps"], 1)
            dve.wait_ge(s["qp_steps"], 6 * j + 3 * t + 2)
            dve.tensor_tensor(k.rotated[t], k.rotated[t], k.swapped[t], ALU.add).then_inc(s["qp_steps"], 1)
            dve.wait_ge(s["hd_unit_hi"], NU * j + n + 1)
            dve.wait_ge(s["qp_steps"], 6 * j + 3 * t + 3)
            lo_part(dve, lo, k.rotated[t], hi).then_inc(s["hd_unit_lo"], 1)
            return
        dve.wait_ge(s["hd_unit_hi"], NU * j + n + 1)
        lo_part(dve, lo, src, hi, k.sm_scale if kind == "qn" else None).then_inc(s["hd_unit_lo"], 1)

    def sample_queries(j):
        dve.wait_ge(s["sq_copied"], 5 * j + 4)
        src = k.ps[:, 7, 0:16].rearrange("p (h b) -> p h b", h=2)
        dve.tensor_scalar(k.sq_nope, src, k.sm_scale, None, ALU.mult).then_inc(s["sq_taken"], 1)
        o = KEPT.at["rope_sample"][0]
        cos, sin = k.kept[:, o:o + 1], k.kept[:, o + 1:o + 2]
        dve.tensor_scalar(k.sq_swapped, k.sq_swapped, sin, k.sm_scale, ALU.mult, ALU.mult).then_inc(s["sq_steps"], 1)
        dve.tensor_scalar(k.sq_rotated, k.ps[:, 7, 16:24], cos, k.sm_scale, ALU.mult, ALU.mult).then_inc(s["sq_steps"], 1)
        dve.wait_ge(s["sq_steps"], 3 * j + 2)
        dve.tensor_tensor(k.sq_rotated, k.sq_rotated, k.sq_swapped, ALU.add).then_inc(s["sq_steps"], 1)
        dve.wait_ge(s["sq_steps"], 3 * j + 3)
        for h in range(2):
            for half in range(2):
                dve.tensor_copy(k.sq_pe_of(j, h, half), k.sq_rotated[64 * h:64 * h + 64, :]).then_inc(s["sq_taken"], 1)

    def sample_latent_queries(j):
        dve.wait_ge(s["sq_done"], 2 * j + 2)
        dve.tensor_copy(k.sq_lat_of(j), k.ps[:, 7, 0:32].rearrange("p (h m b) -> p h m b", h=2, m=2)).then_inc(s["sq_taken"], 1)

    def row_max(j, n):
        i = n % 8
        pieces, w = score_pieces(k, i)
        b0 = SCORE_BANKS[i % 2]
        dve.wait_ge(s["s_done"], 16 * j + n + 1)
        masked = pieces * w - (k.nm + P * i)
        o = KEPT.at["mask"][0]
        last = k.ps[:, b0 + pieces - 1, w - masked:w]
        dve.tensor_tensor(last, last, k.kept[:, o:o + masked], ALU.add).then_inc(s["masked"], 1)
        dve.wait_ge(s["masked"], 16 * j + n + 1)
        dve.tensor_reduce(k.neg_max[:, n % 2:n % 2 + 1], k.ps[:, b0:b0 + pieces, 0:w], AX.XY, ALU.max, negate=True)\
           .then_inc(s["max_done"], 1)

    def normalise(j, n):
        pieces, w = score_pieces(k, n % 8)
        dve.wait_ge(s["exp_done"], 16 * j + n + 1)
        dve.reciprocal(k.row_inv[:, n % 2:n % 2 + 1], k.row_sum[:, n % 2:n % 2 + 1]).then_inc(s["inv"], 1)
        dve.wait_ge(s["inv"], 16 * j + n + 1)
        p = k.probs[:, n % 2, 0:pieces * w]
        dve.tensor_scalar(p, p, k.row_inv[:, n % 2:n % 2 + 1], None, ALU.mult).then_inc(s["p_ready"], 1)

    def turned(j, n):
        for f, fill in enumerate(fills_of(n % 8)):
            g = FILLS_BEFORE[n] + f
            dve.wait_ge(s["pt_hi"], NR * j + RUNS_BEFORE[g + 1])
            for place, slot, count in runs_of(fill):
                src, hi, lo = turned_view(k, g, n, place, slot, count)
                lo_part(dve, lo, src, hi).then_inc(s["pt_lo"], 1)

    dve.wait_ge(s["cols_in"], 16)
    def pair(j, last):
        for n in range(NU):
            unit(j, n)
            if n == 9:
                sample_queries(j)
            if n == 15:
                sample_latent_queries(j)
        for n in range(18):
            if 1 <= n < 17:
                normalise(j, n - 1)
            if n < 16:
                row_max(j, n)
            if n >= 2:
                turned(j, n - 2)

    pairs_of(dve, k, pair)


def heads_pool(pool, k):
    pool.wait_ge(k.s["lat_unit_done"], latent_tasks(k))
    for part in range(2):
        pool.memset(k.pt[:, part, EXTRA_SLOT, 0:P].bitcast(F32), 0.0).then_inc(k.s["extra_zero"], 1)
    heads_split(pool, k, 0, False)
    with pool.Fori(1, k.heads // 2) as j:
        heads_split(pool, k, j, False)


CHUNKS = 8
BAND, BAND_HI, BAND_LO = 184, 56, 120
KEY_BANKS = (0, 1, 2, 7)
SCORE_BANK, VALUE_BANK, SMALL_BANK, PROB_BANK, TAIL_BANK = 3, 4, 5, 6, 7


def page_index_dve(dve, k):
    o = KEPT.at["row_in_block"][0]
    dve.wait_ge(k.s["pages_in"], 16)
    dve.wait_ge(k.s["kept_in"], 16)
    for q in range(4):
        rows = slice(32 * q, 32 * q + 32)
        dve.tensor_scalar(k.block[rows, :], k.pages[rows, q::4], float(32), k.kept[rows, o:o + 1], ALU.mult, ALU.add)\
           .then_inc(k.s["block_ready"], 1)


def decode_steps(eng, step):
    for c in range(CHUNKS):
        step(0, 0, c, True, c >= 1, False)
    for c in range(CHUNKS):
        step(1, 1, c, True, True, c >= 2)
    with eng.Fori(1, 4) as j:
        for par in range(2):
            for c in range(CHUNKS):
                step(2 * j + par, par, c, True, True, True)
    for c in range(CHUNKS):
        step(8, 0, c, False, c == 0, True)
    for c in range(4):
        step(9, 1, c, False, False, c < 2)


def softmax_of(b):
    return not isinstance(b, int) or 1 <= b <= 8


def split_outputs(k, eng, b, c, act):
    if not isinstance(b, int) or b < 8:
        return
    h = c - 2 if b == 8 else c + 6
    if not 0 <= h < k.heads:
        return
    if act:
        if h == 0:
            eng.wait_ge(k.s["dpv_done"], 7 * CHUNKS)
        hi_part(eng, k.xt_hi[:, h, :], k.ot[:, h, :]).then_inc(k.s["o_hi"], 1)
    else:
        eng.wait_ge(k.s["o_hi"], h + 1)
        lo_part(eng, k.xt_lo[:, h, :], k.ot[:, h, :], k.xt_hi[:, h, :]).then_inc(k.s["o_lo"], 1)


def output_of(b):
    return not isinstance(b, int) or 2 <= b <= 9


def decode_sp(sp, k):
    s = k.s
    for slot in range(3):
        sp.wait_ge(s["lat_out%d" % slot], 16 * lat_outs(k, slot))
    sp.wait_ge(s["hd_unit_done"], NU * (k.heads // 2))
    sp.wait_ge(s["s_done"], 8 * k.heads)
    sp.wait_ge(s["qp_steps"], 3 * k.heads)
    sp.dma_start(k.ckv_new, k.ckv_sample[0]).then_inc(s["new_in"], 16)
    with sp.Fori(1, 8) as b:
        sp.wait_ge(s["late_taken"], 2 * b)
        sp.dma_start(k.ckv_new, k.ckv_sample[bass.ds(b, 1), 0, :]).then_inc(s["new_in"], 16)
    sp.wait_ge(s["dc_lo"], k.ns * CHUNKS)
    for r in range(2):
        sp.dma_start(k.value_w[:, r], k.wkv_b[r * P:(r + 1) * P, :, P:2 * P]).then_inc(s["value_w_in"], 16)


def decode_pool(pool, k):
    s = k.s
    ckv = k.cache_ckv.rearrange("g (r i) e -> (g r) (i e)", i=4)
    kpe = k.cache_kpe.rearrange("g (r i) e -> (g r) (i e)", i=4)
    pool.wait_ge(s["pair_w_lo"], k.heads)
    pool.wait_ge(s["sq_done"], k.heads)
    pool.wait_ge(s["sq_taken"], 6 * (k.heads // 2))
    pool.wait_ge(s["filled"], NF * (k.heads // 2))
    pool.wait_ge(s["pv_done"], 4 * k.heads)
    pool.wait_ge(s["s_done"], 8 * k.heads)
    pool.wait_ge(s["block_ready"], 4)
    pool.memset(k.band_q.bitcast(F32), 0.0).then_inc(s["band_zero"], 1)
    pool.memset(k.max_col, 0.0).then_inc(s["band_zero"], 1)
    pool.memset(k.xt_tail.bitcast(F32), 0.0).then_inc(s["band_zero"], 1)

    def load(b, c):
        u = CHUNKS * b + c
        if not isinstance(b, int) or u >= 4:
            pool.wait_ge(s["dc_lo"], u - 3)
        row = k.block_now[:, c % 4:c % 4 + 1]
        pool.tensor_copy(row, k.block[:, bass.ds(u, 1)]).then_inc(s["block_copied"], 1)
        pool.wait_ge(s["block_copied"], u + 1)
        wait_apart(pool, k)
        for src, dst in ((ckv, k.cache_raw(c % 4)[:, 0:1024]), (kpe, k.cache_raw(c % 4)[:, 1024:1280])):
            pool.indirect_dma_start(dst, None, src, bass.IndirectOffsetOnAxis(row, 0))\
                .then_inc(s["cache_in%d" % (c % 4)], 16)

    for c in range(CHUNKS):
        load(0, c)
    with pool.Fori(1, 8) as b:
        for c in range(CHUNKS):
            load(b, c)


def key_part(k, u_c, m):
    w = 256 if m == 2 else 512
    bank = KEY_BANKS[(3 * u_c + m) % 4]
    return k.ps[:, bank, 0:w], k.key_t[:, 0, m * 512:m * 512 + w], k.key_t[:, 1, m * 512:m * 512 + w]


def before_value(b, c):
    vb, vc = (b - 1, c - 2) if c >= 2 else (b - 2, c + 6)
    return vb, vc, CHUNKS * vb + vc


def decode_pe(pe, k):
    s = k.s

    def turn_keys(b, c):
        u = CHUNKS * b + c
        raw = k.cache_raw(c % 4)
        pe.wait_ge(s["cache_in%d" % (c % 4)], 32 * (2 * b + c // 4 + 1))
        for m in range(3):
            q = 3 * u + m
            if not isinstance(q, int) or q >= 4:
                pe.wait_ge(s["kt_lo"], q - 3)
            ps = key_part(k, c, m)[0]
            for i in range(2 if m == 2 else 4):
                src = raw[:, 1024 + i * P:1024 + (i + 1) * P] if m == 2 else raw[:, i * 256 + m * P:i * 256 + (m + 1) * P]
                mm = pe.transpose(ps[:, i * P:(i + 1) * P], src, k.ident)
            mm.then_inc(s["kt_turned"], 1)

    def scores(b, c):
        u = CHUNKS * b + c
        if c == 0:
            pe.wait_ge(s["band_lo"], b + 1)
            if not isinstance(b, int) or b:
                pe.wait_ge(s["ds_taken"], b)
        win = slice(BAND_HI - 8 * c, BAND_HI - 8 * c + P)
        out = k.ps[:, SCORE_BANK, :]
        for m in range(3):
            pe.wait_ge(s["kt_lo"], 3 * u + m + 1)
            _, hi, lo = key_part(k, c, m)
            if m < 2:
                pe.matmul(out, k.band_q[:, m, win], hi, start=c == 0 and m == 0, stop=False)
                mm = pe.matmul(out, k.band_q[:, m, win], lo, start=False, stop=False)
            else:
                for par in range(2):
                    part = out.rearrange("p (m a n) -> p m a n", m=2, a=2)[:, :, par, :]
                    for x in (hi, lo):
                        mm = pe.matmul(part, k.band_q[:, 2 + par, win], x.rearrange("p (m n) -> p m n", m=2),
                                       start=False, stop=c == CHUNKS - 1 and par == 1 and x is lo)
            mm.then_inc(s["kt_used"], 1)

    def values(b, par, c):
        vb, vc, v = before_value(b, c)
        slot = 1 - par if c >= 2 else par
        if vc == 0:
            pe.wait_ge(s["dpt_lo"], vb + 1)
            if not isinstance(vb, int) or vb:
                pe.wait_ge(s["do_steps"], 4 * vb)
        pe.wait_ge(s["dc_lo"], v + 1)
        for i in range(4):
            mm = pe.matmul(k.ps[0:72, VALUE_BANK, :], k.prob_t[:, i, 8 * vc:8 * vc + 72], k.values[:, slot, vc, i, :],
                           start=vc == 0 and i == 0, stop=vc == CHUNKS - 1 and i == 3)
        mm.then_inc(s["dpv_done"], 1)

    def new_scores():
        pe.wait_ge(s["sq_taken"], 6 * (k.heads // 2))
        pe.wait_ge(s["exp_done"], 8 * k.heads)
        pe.wait_ge(s["pt_lo"], NR * (k.heads // 2))
        pe.wait_ge(s["o_copied"], 4 * k.heads)
        pe.wait_ge(s["band_zero"], 3)
        for b in range(k.ns):
            for m in range(3):
                rows = slice(0, 64 if m == 2 else P)
                mm = pe.matmul(k.ps[0:1, SMALL_BANK, 8 * b:8 * b + 8], k.lat_s[rows, m, b:b + 1], k.q_all[rows, :, m, b],
                               start=m == 0, stop=m == 2)
        mm.then_inc(s["small"], 1)

    def small(b, n):
        return 1 + 3 * b + n

    def max_row(b):
        pe.wait_ge(s["row_max"], b + 1)
        if not isinstance(b, int) or b:
            pe.wait_ge(s["late_taken"], 2 * b)
        pe.matmul(k.ps[:, SMALL_BANK, 0:64], k.max_col, k.ident[0:64, 0:64], start=True, stop=True)\
          .then_inc(s["small"], 1)

    def max_spread(b):
        pe.wait_ge(s["max_tiled"], b + 1)
        wait_apart(pe, k)
        pe.matmul(k.ps[0:64, SMALL_BANK, 64:65], k.max_tile, k.one[0:1], start=True, stop=True).then_inc(s["small"], 1)

    def turn_probs(b):
        pe.wait_ge(s["dexp"], b + 1)
        if not isinstance(b, int) or b:
            pe.wait_ge(s["dpt_lo"], b)
        wait_apart(pe, k)
        for i in range(4):
            mm = pe.transpose(k.ps[:, PROB_BANK, i * 64:(i + 1) * 64], k.probs_s[:, i * P:(i + 1) * P], k.ident[0:64, 0:64])
        mm.then_inc(s["dp_turned"], 1)

    def late(b):
        pe.wait_ge(s["new_p"], b + 1)
        pe.wait_ge(s["neg_taken"], b + 1)
        if output_of_late(b):
            pe.wait_ge(s["out_taken"], b)
        pe.wait_ge(s["new_in"], 16 * (b + 1))
        wait_apart(pe, k)
        o = KEPT.at["same_head"][0]
        pe.matmul(k.ps[0:8, SMALL_BANK, 65:66], k.kept[0:64, o:o + 8], k.exp_sum, start=True, stop=False)
        pe.matmul(k.ps[0:8, SMALL_BANK, 65:66], k.new_p, k.one[0:1], start=False, stop=True)
        pe.matmul(k.ps[0:8, SMALL_BANK, 256:512], k.new_p, k.ckv_new, start=True, stop=True)\
          .then_inc(s["small"], 1)

    def output_of_late(b):
        return not isinstance(b, int) or b >= 1

    def turn_output(b):
        pe.wait_ge(s["out_norm"], b + 1)
        wait_apart(pe, k)
        for r in range(2):
            mm = pe.transpose(k.ps[:, SMALL_BANK, 80 + 8 * r:88 + 8 * r], k.out_rows[:, r * P:(r + 1) * P], k.ident[0:8, 0:8])
        mm.then_inc(s["out_turned"], 1)

    new_scores()

    def step(b, par, c, keys, sc, va):
        if keys:
            turn_keys(b, c)
        if c == 2 and softmax_of(b):
            turn_probs(b - 1)
        if sc:
            if c == 0:
                scores(b - 1, CHUNKS - 1)
            elif keys:
                scores(b, c - 1)
        if c == 1 and softmax_of(b):
            max_row(b - 1)
        if va:
            values(b, par, c)
        if c == 1 and softmax_of(b):
            max_spread(b - 1)
        if c == 3 and output_of(b):
            turn_output(b - 2)
        if c == 3 and softmax_of(b):
            late(b - 1)

    decode_steps(pe, step)

    pe.wait_ge(s["out_taken"], k.ns)
    pe.wait_ge(s["value_w_in"], 32)
    for h in range(k.heads):
        for r in range(2):
            mm = pe.matmul(k.ps[:, TAIL_BANK, 8 * h:8 * h + 8], k.value_w[:, r, h, :], k.out_lat[:, :, r, h],
                           start=r == 0, stop=r == 1)
    mm.then_inc(s["tail_out"], 1)


def decode_act(act, k):
    s = k.s

    def step(b, par, c, keys, sc, va):
        def key_hi(m):
            u = CHUNKS * b + c
            act.wait_ge(s["kt_turned"], 3 * u + m + 1)
            if not isinstance(u, int) or u >= 1:
                act.wait_ge(s["kt_used"], 3 * (u - 1) + m + 1)
            src, hi, _ = key_part(k, c, m)
            hi_part(act, hi, src).then_inc(s["kt_hi"], 1)

        if keys:
            key_hi(0)
        if c == 2 and softmax_of(b):
            act.wait_ge(s["dp_turned"], b)
            if not isinstance(b, int) or b >= 2:
                act.wait_ge(s["dpv_done"], CHUNKS * (b - 1))
            hi_part(act, k.prob_t[:, :, 0:64], k.ps[:, PROB_BANK, 0:256].rearrange("p (i n) -> p i n", i=4))\
                .then_inc(s["dpt_hi"], 1)
        if keys:
            key_hi(1)
            key_hi(2)
        if c == 0 and keys:
            if not isinstance(b, int) or b:
                act.wait_ge(s["kt_used"], 3 * CHUNKS * b)
            hi_part(act, k.band_q[:, :, BAND_HI:BAND_HI + 8], k.q_of(b)).then_inc(s["band_hi"], 1)
        if c == 0 and softmax_of(b):
            act.wait_ge(s["kt_used"], 3 * CHUNKS * b)
            act.activation(k.scores_s, k.ps[0:64, SCORE_BANK, :], ACT.Copy).then_inc(s["ds_steps"], 1)
        if c == 1 and softmax_of(b):
            act.wait_ge(s["neg_taken"], b)
            if not isinstance(b, int) or b >= 2:
                act.wait_ge(s["late_taken"], 2 * (b - 1))
            act.activation(k.probs_s, k.scores_s, ACT.Exp, bias=k.neg_m, scale=1.0, accum_out=k.exp_sum)\
               .then_inc(s["dexp"], 1)
        if c == 2 and softmax_of(b):
            act.wait_ge(s["new_d"], b)
            act.activation(k.new_p, k.new_diff, ACT.Exp).then_inc(s["new_p"], 1)
        if keys:
            v = CHUNKS * b + c
            if not isinstance(v, int) or v >= 2 * CHUNKS:
                act.wait_ge(s["dpv_done"], v - 2 * CHUNKS + 1)
            act.wait_ge(s["cache_in%d" % (c % 4)], 32 * (2 * b + c // 4 + 1))
            hi_part(act, k.values[:, par, c, :, 0:256], k.cache_raw(c % 4)[:, 0:1024].rearrange("p (i e) -> p i e", i=4))\
                .then_inc(s["dc_hi"], 1)
        split_outputs(k, act, b, c, True)

    act.wait_ge(s["o_copied"], 4 * k.heads)
    act.wait_ge(s["band_zero"], 3)
    act.wait_ge(s["sq_taken"], 6 * (k.heads // 2))
    decode_steps(act, step)


def decode_dve(dve, k):
    s = k.s

    def step(b, par, c, keys, sc, va):
        def key_lo(m):
            dve.wait_ge(s["kt_hi"], 3 * (CHUNKS * b + c) + m + 1)
            src, hi, lo = key_part(k, c, m)
            lo_part(dve, lo, src, hi).then_inc(s["kt_lo"], 1)

        if keys:
            key_lo(0)
        if c == 1 and softmax_of(b):
            dve.wait_ge(s["small"], 1 + 3 * (b - 1) + 1)
            dve.tensor_reduce(k.max_head, k.ps[0:1, SMALL_BANK, 0:64].rearrange("p (c h) -> p h c", c=CHUNKS), AX.X,
                              ALU.max).then_inc(s["dmax_steps"], 1)
            dve.wait_ge(s["dmax_steps"], b)
            tile = k.max_tile.rearrange("p (c h) -> p c h", c=CHUNKS)
            dve.tensor_tensor(tile, k.max_head.unsqueeze(1).to_broadcast([1, CHUNKS, 8]),
                              k.new_s[:, bass.ts(b - 1, 8)].unsqueeze(1).to_broadcast([1, CHUNKS, 8]), ALU.max)\
               .then_inc(s["max_tiled"], 1)
        if c == 2 and softmax_of(b):
            dve.wait_ge(s["dpt_hi"], b)
            lo_part(dve, k.prob_t[:, :, 64:128], k.ps[:, PROB_BANK, 0:256].rearrange("p (i n) -> p i n", i=4),
                    k.prob_t[:, :, 0:64]).then_inc(s["dpt_lo"], 1)
        if keys:
            key_lo(1)
            key_lo(2)
        if c == 0 and keys:
            dve.wait_ge(s["band_hi"], b + 1)
            lo_part(dve, k.band_q[:, :, BAND_LO:BAND_LO + 8], k.q_of(b), k.band_q[:, :, BAND_HI:BAND_HI + 8])\
                .then_inc(s["band_lo"], 1)
        if c == 0 and softmax_of(b):
            dve.wait_ge(s["ds_steps"], b)
            dve.tensor_tensor(k.scores_s, k.scores_s, k.ps[64:128, SCORE_BANK, :], ALU.add).then_inc(s["ds_taken"], 1)
            dve.wait_ge(s["ds_taken"], b)
            dve.tensor_reduce(k.max_col[:, 0:1], k.scores_s, AX.X, ALU.max).then_inc(s["row_max"], 1)
        if c == 1 and softmax_of(b):
            dve.wait_ge(s["small"], 1 + 3 * (b - 1) + 2)
            dve.tensor_scalar(k.neg_m, k.ps[0:64, SMALL_BANK, 64:65], -1.0, None, ALU.mult).then_inc(s["neg_taken"], 1)
            if not isinstance(b, int) or b > 1:
                dve.wait_ge(s["new_p"], b - 1)
            dve.wait_ge(s["max_tiled"], b)
            dve.tensor_tensor(k.new_diff, k.new_s[:, bass.ts(b - 1, 8)], k.max_tile[:, 0:8], ALU.subtract)\
               .then_inc(s["new_d"], 1)
        if c == 2 and output_of(b):
            dve.wait_ge(s["dpv_done"], CHUNKS * (b - 1))
            ps = k.ps[:, VALUE_BANK, :]
            dve.wait_ge(s["late_taken"], 2 * (b - 1))
            base = 4 * (b - 2)
            rows = k.out_rows

            def add(part, n):
                dve.wait_ge(s["do_steps"], base + n)
                return dve.tensor_tensor(rows, rows, part, ALU.add)

            dve.tensor_tensor(rows, k.new_out, ps[0:8, 0:256], ALU.add).then_inc(s["do_steps"], 1)
            add(ps[0:8, 256:512], 1).then_inc(s["do_steps"], 1)
            add(ps[64:72, 0:256], 2).then_inc(s["do_steps"], 1)
            add(ps[64:72, 256:512], 3).then_inc(s["do_steps"], 1)
            dve.wait_ge(s["do_steps"], base + 4)
            dve.tensor_scalar(rows, rows, k.sum_inv, None, ALU.mult).then_inc(s["out_norm"], 1)
        if c == 3 and output_of(b):
            dve.wait_ge(s["out_turned"], b - 1)
            dve.tensor_copy(k.out_of(b - 2), k.ps[:, SMALL_BANK, 80:96]).then_inc(s["out_taken"], 1)
        if c == 3 and softmax_of(b):
            dve.wait_ge(s["small"], 1 + 3 * (b - 1) + 3)
            dve.reciprocal(k.sum_inv, k.ps[0:8, SMALL_BANK, 65:66]).then_inc(s["late_taken"], 1)
            dve.tensor_copy(k.new_out, k.ps[0:8, SMALL_BANK, 256:512]).then_inc(s["late_taken"], 1)
        if keys:
            dve.wait_ge(s["dc_hi"], CHUNKS * b + c + 1)
            lo_part(dve, k.values[:, par, c, :, 256:512], k.cache_raw(c % 4)[:, 0:1024].rearrange("p (i e) -> p i e", i=4),
                    k.values[:, par, c, :, 0:256]).then_inc(s["dc_lo"], 1)
        split_outputs(k, dve, b, c, False)

    dve.wait_ge(s["small"], 1)
    dve.tensor_copy(k.new_s, k.ps[0:1, SMALL_BANK, 0:64]).then_inc(s["new_s"], 1)
    dve.wait_ge(s["new_s"], 1)
    decode_steps(dve, step)


def samples_operand(dve, k):
    s = k.s
    dve.wait_ge(s["tail_out"], 1)
    src = k.ps[:, TAIL_BANK, 0:64].rearrange("p (h b) -> p h b", h=k.heads)
    dve.tensor_copy(k.xt_tail[:, :, 0:k.ns], src).then_inc(s["o_tail"], 1)
    dve.wait_ge(s["o_tail"], 1)
    lo_part(dve, k.xt_tail[:, :, LO:LO + k.ns], src, k.xt_tail[:, :, 0:k.ns]).then_inc(s["o_tail"], 1)


def project_sp(sp, k):
    s = k.s
    sp.wait_ge(s["dc_lo"], k.ns * CHUNKS)
    for c in range(k.heads):
        if c >= 3:
            sp.wait_ge(s["wo_lo"], c - 2)
        sp.dma_start(k.raw[:, c % 3, :], k.wo_w[0, c * P:(c + 1) * P, :]).then_inc(s["wo_in%d" % (c % 3)], 16)
    x = k.x_spill.rearrange("(t p) d -> p t d", p=P)
    sp.wait_ge(s["o_lo"], k.heads)
    for t in range(k.tiles):
        sp.dma_start(k.x_main[:, t, :], x[:, t, :]).then_inc(s["x_back%d" % t], 16)
    sp.wait_ge(s["tail_out"], 1)
    sp_load_gain(sp, k, "att", 1, 0)


def project_split(eng, k, act):
    s = k.s
    for c in range(k.heads):
        if act:
            eng.wait_ge(s["wo_in%d" % (c % 3)], 16 * (c // 3 + 1))
            hi_part(eng, k.wo[:, 0, c, :], k.raw[:, c % 3, :]).then_inc(s["wo_hi"], 1)
        else:
            eng.wait_ge(s["wo_hi"], c + 1)
            lo_part(eng, k.wo[:, 1, c, :], k.raw[:, c % 3, :], k.wo[:, 0, c, :]).then_inc(s["wo_lo"], 1)


def project_pe(pe, k):
    s, ns = k.s, k.ns

    def units(t):
        for e in range(2):
            u = 2 * t + e
            if u == 0:
                pe.wait_ge(s["o_lo"], k.heads)
            if u == 2 * k.tiles:
                pe.wait_ge(s["o_tail"], 2)
            pe_unit_free(pe, k, "att", u)
            out, cols = k.ps[:, unit_bank(u), :], slice(e * BANK, (e + 1) * BANK)
            for c in range(k.heads):
                if u == 0:
                    pe.wait_ge(s["wo_lo"], c + 1)
                w = (k.wo[:, 0, c, cols], k.wo[:, 1, c, cols])
                if t < k.tiles:
                    rows = slice(t * P, (t + 1) * P)
                    mm = product(pe, out, (k.xt_hi[:, c, rows], k.xt_lo[:, c, rows]), w, c == 0, c == k.heads - 1)
                else:
                    mm = product_tail(pe, out[0:LO + ns], k.xt_tail[:, c, 0:LO + ns], w, c == 0, c == k.heads - 1)
            mm.then_inc(s["att_unit_done"], 1)

    pe_norm_stage(pe, k, "att", ns, units, True, first_gate_up(k, pe, 1))


def project_act(act, k):
    act.wait_ge(k.s["dpv_done"], k.ns * CHUNKS)
    project_split(act, k, True)
    act_norm_stage(act, k, "att", k.ns, True, first_weights(k, act, 1, True))


def project_dve(dve, k):
    weights = first_weights(k, dve, 1, False)

    def rows_back(step):
        weights(step)
        if step < k.tiles:
            dve.wait_ge(k.s["x_back%d" % step], 16)

    project_split(dve, k, False)
    samples_operand(dve, k)
    dve_norm_stage(dve, k, "att", k.ns, True, True, extra=rows_back)


def trunk(nc, k):
    k.ns, k.nm = k.x_sample.shape[0], k.meta_tokens.shape[0]
    k.seq, k.d = k.x_prompt.shape[1:]
    k.tiles, k.kc = k.seq // P, k.d // P
    k.ff = k.w_gate.shape[2]
    k.rank, k.rope, k.heads = k.kv_norm.shape[0], k.cache_kpe.shape[2], k.wkv_b.shape[1]
    k.kv_w, k.q_w = k.rank + k.rope, k.wq_a.shape[2]
    k.head_q, k.head_kv = k.wq_b.shape[2] // k.heads, k.wkv_b.shape[2]
    k.sm_scale = float(k.head_q ** -0.5)
    k.x_spill = nc.dram_tensor("x_spill", (k.seq, k.d), F32, kind="Internal").ap()
    nt = k.ns + k.nm
    k.n_stored = 0
    with ExitStack() as ctx:
        sb = lambda name, shape, dt: ctx.enter_context(nc.sbuf_tensor(name, shape, dt))
        k.s = Sems(ctx, nc, k.tiles, k.ff // (2 * P))
        R_SIZE, TW = 36864, LO + nt
        split = sb("split", [P, R_SIZE + (k.kc + 4) * TW], F32R)
        plain = sb("plain", [P, 18260], F32)
        k.ps = ctx.enter_context(nc.psum_tensor("ps", [P, 8, BANK], F32))

        def cut(t, at, *dims):
            n = int(np.prod(dims))
            v = t[:, at:at + n]
            names = "abcde"[:len(dims)]
            return v.rearrange("p (%s) -> p %s" % (" ".join(names), " ".join(names)),
                               **{x: y for x, y in zip(names[:-1], dims[:-1])}) if len(dims) > 1 else v

        k.split, k.plain, k.cut = split, plain, cut
        k.xt_hi, k.xt_lo = cut(split, 0, k.kc, k.seq), cut(split, 8192, k.kc, k.seq)
        k.wgu = cut(split, 16384, 2, 2, 2, k.kc, P)
        k.wgu_first = cut(split, 32768, 2, 2, k.kc, P)
        k.wd = cut(split, 24576, 2, 2, k.d)
        k.h = cut(split, 28672, 2, 2, 2, k.seq)
        k.xt_tail = cut(split, R_SIZE, k.kc, TW)
        k.h_tail = cut(split, R_SIZE + k.kc * TW, 2, 2, TW)
        k.pooled_hi, k.pooled_lo = cut(split, 24576, 2, k.kc, P), cut(split, 26624, 2, k.kc, P)
        k.pool_hi, k.pool_lo = cut(split, 28672, k.kc, 256), cut(split, 30720, k.kc, 256)
        k.pooled_tail = cut(split, 32768, k.kc, TW)
        k.x_main = cut(plain, 0, k.tiles, k.d)
        k.raw = cut(plain, 8192, 3, 1024)
        k.pool_raw, k.hist = cut(plain, 8192, k.kc, 256), cut(plain, 8192 + 2048, 1024)
        TMP = 11264
        k.silu, k.hidden = cut(plain, TMP, 2, BANK), cut(plain, TMP + 1024, 2, BANK)
        bl = bands_layout(nt)
        k.bands = cut(plain, TMP, bl.width)
        GB = TMP + 2112
        k.gain, k.bias = cut(plain, GB, k.d), cut(plain, GB + 1024, k.d)
        k.x_tail = cut(plain, GB + 2048, k.d)
        KEEP = GB + 3072
        k.kept = cut(plain, KEEP, KEPT.width)
        M1 = KEEP + KEPT.width
        k.pool_gain = cut(plain, M1, k.d)
        M2 = M1 + 1024
        k.tail_gu, k.tail_silu, k.tail_h = cut(plain, M1, 512), cut(plain, M1 + 512, 256), cut(plain, M1 + 768, 256)
        k.stats, k.mean_var = cut(plain, M2, 2, 2, 6), cut(plain, M2 + 24, k.tiles + 1, 2)
        smalls = ["root", "var_eps", "scale", "shift", "newton"]
        k.root, k.var_eps, k.scale, k.shift, k.newton = (cut(plain, M2 + 42 + 9 * i, k.tiles + 1) for i in range(5))
        k.ln_eps, k.rms_eps = cut(plain, M2 + 87, 1), cut(plain, M2 + 88, 1)
        k.m3 = M2 + 89
        kva, cqa = cut(split, 16384, 2, k.kc, k.kv_w), cut(split, 16384, 2, 6, k.q_w)
        cqb = cut(split, 16384 + 2 * k.kc * k.kv_w, 2, 2, k.q_w)

        def lat_w(n):
            if n < 4:
                return [kva[:, q, 2 * n:2 * n + 2, :] for q in range(2)]
            if n == 4:
                return [cqb[:, q] for q in range(2)]
            return [cqa[:, q, 2 * (n - 5):2 * (n - 5) + 2, :] for q in range(2)]

        k.lat_w = lat_w
        k.lat_raw = lambda n: cut(plain, 8192 + 768 * (n % 4), 2, k.kv_w if n < 4 else k.q_w)
        k.keys = -(-(k.nm + k.seq) // (3 * 32)) * 96
        LAT = R_SIZE - 2 * 6 * k.keys
        k.lat = cut(split, LAT, 2, 6, k.keys)
        k.lat_in, k.lat_row = cut(plain, TMP, 2, 384), cut(plain, TMP + 768, 3, 384)
        k.rope_rows = cut(plain, GB, k.tiles + 1, 2 * k.rope)
        k.kv_gain, k.q_gain = cut(plain, GB + 1152, k.rank), cut(plain, GB + 1152 + 256, k.q_w)
        k.rope_tmp = cut(plain, M1, k.rope)
        k.lat_ss, k.lat_root, k.lat_var, k.lat_scale, k.lat_newton = \
            (cut(plain, M1 + 64 + 18 * i, latent_tasks(k)) for i in range(5))
        k.lat_s = cut(plain, k.m3, 6, k.ns)
        QL = k.m3 + 6 * k.ns
        at = [0]

        def take(*dims):
            v = cut(split, at[0], *dims)
            at[0] += int(np.prod(dims))
            return v

        k.wq, k.wkv = take(2, 3, 2 * k.head_q), take(2, 2, 2 * k.head_kv)
        k.qp, k.qn, k.kn = take(2, k.seq), take(2, 2, k.seq), take(2, 2, k.keys)
        k.v, k.pt = take(2, 9, 256), take(2, 9, 256)
        assert at[0] <= LAT
        k.wq_raw, k.wkv_raw = cut(plain, 8192, 3, 2 * k.head_q), cut(plain, 8192 + 1152, 2, 2 * k.head_kv)
        k.wkv_v = lambda q, c: k.wkv[:, q, c, :].rearrange("p (h e) -> p h e", h=2)[:, :, P:2 * P]
        k.key_w = cut(plain, 8192 + 2176, 4, P)
        k.sq_nope = cut(plain, 8192 + 2176 + 512, 2, 8)
        k.sq_swapped, k.sq_rotated = cut(plain, 8192 + 2704, 8), cut(plain, 8192 + 2712, 8)
        k.neg_max, k.row_sum, k.row_inv = (cut(plain, M2 + 2 * i, 2) for i in range(3))
        k.probs = cut(plain, TMP, 2, k.keys)
        k.rope_cols = cut(plain, GB, 2, k.seq)
        k.swapped, k.rotated = [[cut(plain, a + b, BANK) for a in (M1, TMP)] for b in (0, BANK)]
        k.q_all = cut(plain, QL, k.heads, 4, 8)
        k.sq_lat_of = lambda j: plain[:, bass.ds(QL + 64 * j, 64)].rearrange("p (h m b) -> p h m b", h=2, m=4)[:, :, 0:2, :]
        k.sq_pe_of = lambda j, h, half: plain[64 * half:64 * half + 64, bass.ds(QL + 64 * j + 32 * h + 16 + 8 * half, 8)]
        k.q_of = lambda b: k.q_all.rearrange("p h m b -> p m h b")[:, :, :, b] if isinstance(b, int) else \
            k.q_all.rearrange("p h m b -> p m h b")[:, :, :, bass.ds(b, 1)].rearrange("p m h b -> p m (h b)")
        k.ot = cut(plain, 0, k.heads, k.seq)
        k.ot_of = lambda j, h: plain[:, bass.ds(2 * k.seq * j + k.seq * h, k.seq)]
        k.wo = cut(split, 16384, 2, k.heads, k.d)
        at[0] = 0
        k.values, k.key_t, k.band_q, k.prob_t = take(2, CHUNKS, 4, 512), take(2, 1280), take(4, BAND), take(4, P)
        assert at[0] <= R_SIZE
        at = [GB]

        def take_plain(*dims):
            v = cut(plain, at[0], *dims)
            at[0] += int(np.prod(dims))
            return v

        k.ckv_new, k.max_col = take_plain(k.rank)[0:1], take_plain(P)[0:64]
        k.new_out, k.out_rows = take_plain(256)[0:8], take_plain(256)[0:8]
        out_at = at[0]
        k.out_lat = take_plain(k.ns, 2, k.heads)
        k.out_of = lambda b: plain[:, bass.ds(out_at + 16 * b, 16)]
        k.max_head, k.max_tile, k.new_s = take_plain(8)[0:1], take_plain(64)[0:1], take_plain(64)[0:1]
        k.new_diff, k.new_p = take_plain(8)[0:1], take_plain(8)[0:1]
        k.neg_m, k.exp_sum, k.sum_inv = take_plain(1)[0:64], take_plain(1)[0:64], take_plain(1)[0:8]
        assert at[0] <= GB + 2048
        k.scores_s, k.probs_s = cut(plain, M1, BANK)[0:64], cut(plain, M1 + BANK, BANK)[0:64]
        k.value_w = cut(plain, TMP, 2, k.heads, P)
        k.cache_raw = lambda slot: cut(plain, 8192 + 1280 * slot, 1280)
        k.one = k.kept[:, KEPT.at["one"][0]:KEPT.at["one"][0] + 1]
        k.block, k.block_now = sb("block", [P, 8 * CHUNKS], I32)[:, :], sb("block_now", [P, 4], I32)[:, :]
        k.pages = cut(plain, k.m3, 256).bitcast(I32)
        k.ident = k.kept[:, KEPT.at["ident"][0]:KEPT.at["ident"][0] + P]

        def band(name, g):
            o, w = bl.at[name]
            n = w // len(WINDOWS)
            return k.bands[:, o + g * n:o + (g + 1) * n]

        k.pool_band = band
        ffn = k.ffn = [Ffn(k, 0, nt), Ffn(k, 1, k.ns)]
        block = ctx.enter_context(nc.Block())

        @block.sync
        def _(sp):
            mixer_sp(sp, k)
            ffn[0].sp(sp)
            latent_sp(sp, k)
            heads_sp(sp, k)
            decode_sp(sp, k)
            project_sp(sp, k)
            sp.wait_ge(k.s["wo_lo"], k.heads)
            ffn[1].sp(sp)
            results_sp(sp, k)
            sp.wait_ge(k.s["stored"], 16 * k.n_stored)

        @block.tensor
        def _(pe):
            mixer_pe(pe, k)
            ffn[0].pe(pe)
            latent_pe(pe, k)
            heads_pe(pe, k)
            decode_pe(pe, k)
            project_pe(pe, k)
            ffn[1].pe(pe)

        @block.scalar
        def _(act):
            act.wait_ge(k.s["zeroed"], 2)
            act.wait_ge(k.s["pads"], 4)
            mixer_act(act, k)
            ffn[0].act(act)
            latent_act(act, k)
            heads_act(act, k)
            decode_act(act, k)
            project_act(act, k)
            ffn[1].act(act)

        @block.vector
        def _(dve):
            page_index_dve(dve, k)
            mixer_dve(dve, k)
            ffn[0].dve(dve)
            latent_dve(dve, k)
            heads_dve(dve, k)
            decode_dve(dve, k)
            project_dve(dve, k)
            ffn[1].dve(dve)

        @block.gpsimd
        def _(pool):
            mixer_pool(pool, k)
            ffn[0].pool(pool)
            latent_pool(pool, k)
            heads_pool(pool, k)
            decode_pool(pool, k)
            pool_norm_stage(pool, k, "att", k.ns)
            ffn[1].pool(pool)


_INS = ["x_prompt", "x_sample", "state_pool", "cache_ckv", "cache_kpe", "page_table", "meta_tokens",
        "ln_g", "ln_b", "pool_w", "pool_scale", "w_gate", "w_up", "w_down",
        "wq_a", "q_norm", "wq_b", "wo", "wkv_a", "kv_norm", "wkv_b"]
_OUTS = ["y_prompt", "y_sample", "pool_prompt", "pool_sample", "ckv_prompt", "kpe_prompt", "ckv_sample", "kpe_sample"]


def shapes_and_constants(a):
    b, seq, d = a["x_prompt"].shape
    ns = a["x_sample"].shape[0]
    nm = a["meta_tokens"].shape[0]
    kv = a["kv_norm"].shape[0]
    rope = a["cache_kpe"].shape[2]
    page = a["cache_ckv"].shape[1]
    past = a["page_table"].shape[1] * page
    heads = a["wkv_b"].shape[1]
    nope = a["wq_b"].shape[2] // heads - rope
    scale = (nope + rope) ** -0.5
    outs = [(b, seq, d), (ns, 1, d), (1, b, 15, d), (1, ns, 15, d), (b, seq + nm, kv), (b, seq + nm, rope),
            (ns, 1, kv), (ns, 1, rope)]
    consts = {"in_kept": kept_constants(heads, ns, past, rope // 2, scale),
              "in_bands": band_constants(ns, nm),
              "in_rope_rows": rope_rows(seq, ns, nm, past, rope // 2),
              "in_rope_cols": rope_columns(seq, nm, rope // 2, scale)}
    return outs, consts


def make(nc, arrays_in, outs):
    drams = {name: nc.dram_tensor(name, a.shape, mybir.dt.from_np(a.dtype), kind="ExternalInput").ap()
             for name, a in arrays_in.items()}
    drams.update({name: nc.dram_tensor(name, shape, F32, kind="ExternalOutput").ap()
                  for name, shape in zip(_OUTS, outs)})
    k = Shared(drams)
    trunk(nc, k)


def kernel(**inputs):
    import concourse.bacc as bacc
    from concourse.bass_utils import run_bass_kernel_spmd

    arrays = {n: np.ascontiguousarray(inputs[n]) for n in _INS}
    outs, consts = shapes_and_constants(arrays)
    arrays.update(consts)
    nc = bacc.Bacc("TRN2", target_bir_lowering=False, num_devices=1, dynamic_dma_scratch_size=4096)
    make(nc, arrays, outs)
    r = run_bass_kernel_spmd(nc, [arrays], core_ids=[0])
    return tuple(r.results[0][n] for n in _OUTS)
```
